# Optimizing a Trainium2 kernel written in Bass

```python
import math
import jax
import jax.numpy as jnp
from jax import lax
import numpy as np

D_MODEL = 1024
BATCH = 1
SEQ = 256
DEPTH = 2
DEC_BATCH = 8
DEC_SEQ = 4
PAST_LEN = 2048
PAGE_SIZE = 128

N_MIXERS = 2
N_GLA_LAYERS = (DEPTH + 1) // 2
N_MLSTM_LAYERS = DEPTH // 2
N_DENSE_LAYERS = (DEPTH + 1) // 2
N_MOE_LAYERS = DEPTH // 2

QK_W = D_MODEL // 2
V_W = D_MODEL

GLA_HEADS = 4
GLA_DK = QK_W // GLA_HEADS
GLA_DV = V_W // GLA_HEADS
GLA_RANK = 16
GLA_TAU = 16.0
GLA_IN = 2 * QK_W + 2 * V_W + GLA_RANK

MLSTM_HEADS = 8
MLSTM_DK = QK_W // MLSTM_HEADS
MLSTM_DV = V_W // MLSTM_HEADS
GATE_CAP = 15.0
FORGET_BIAS = 3.0
MLSTM_IN = 2 * QK_W + 2 * V_W + 2 * MLSTM_HEADS

CHUNK = 64
D_FF = 2816
N_EXPERTS = 8
TOP_K = 2
D_FF_EXPERT = 3584
EPS = 1e-6
F32 = jnp.float32

kernel_name = 'gla_mlstm_hybrid_moe_decode_step'

def rms_norm(x, g):
    xf = x.astype(F32)
    y = xf * lax.rsqrt(jnp.mean(xf * xf, axis=-1, keepdims=True) + EPS)
    return (y * g.astype(F32)).astype(x.dtype)

def chunk_len(t):
    return math.gcd(t, CHUNK)

def split_chunks(a, L):
    b, t, h, d = a.shape
    return a.reshape(b, t // L, L, h, d).transpose(1, 0, 3, 2, 4)

def split_gate_chunks(a, L):
    b, t, h = a.shape
    return a.reshape(b, t // L, L, h).transpose(1, 0, 3, 2)

def merge_chunks(a):
    nc, b, h, L, d = a.shape
    return a.transpose(1, 0, 3, 2, 4).reshape(b, nc * L, h, d)

def gla_recurrence(q, k, v, log_a, S0):
    L = chunk_len(q.shape[1])
    causal = jnp.tril(jnp.ones((L, L), dtype=bool))

    def step(S, blk):
        qi, ki, vi, gi = blk
        b = jnp.cumsum(gi, axis=2)
        qg = qi * jnp.exp(b)
        kg = ki * jnp.exp(-b)
        A = jnp.where(causal, jnp.einsum('bhtd,bhsd->bhts', qg, kg), 0.0)
        o = jnp.einsum('bhtd,bhdv->bhtv', qg, S) + jnp.einsum('bhts,bhsv->bhtv', A, vi)
        b_end = b[:, :, -1:, :]
        k_end = ki * jnp.exp(b_end - b)
        S_new = jnp.exp(b_end[:, :, 0, :])[..., None] * S + jnp.einsum('bhsd,bhsv->bhdv', k_end, vi)
        return S_new, o

    S_T, o = lax.scan(step, S0, (split_chunks(q, L), split_chunks(k, L),
                                 split_chunks(v, L), split_chunks(log_a, L)))
    return merge_chunks(o), S_T

def mlstm_recurrence(q, k, v, i_pre, log_f, C0, n0, m0):
    L = chunk_len(q.shape[1])
    causal = jnp.tril(jnp.ones((L, L), dtype=bool))

    def step(carry, blk):
        C, n, m = carry
        qi, ki, vi, ii, fi = blk
        F = jnp.cumsum(fi, axis=-1)
        D = jnp.where(causal, F[..., :, None] - F[..., None, :] + ii[..., None, :], -jnp.inf)
        inter = F + m[..., None]
        m_t = jnp.maximum(inter, jnp.max(D, axis=-1))
        w_inter = jnp.exp(inter - m_t)
        S = jnp.einsum('bhtd,bhsd->bhts', qi, ki) * jnp.exp(D - m_t[..., None])
        num = w_inter[..., None] * jnp.einsum('bhtd,bhdv->bhtv', qi, C) + jnp.einsum('bhts,bhsv->bhtv', S, vi)
        den = w_inter * jnp.einsum('bhtd,bhd->bht', qi, n) + jnp.sum(S, axis=-1)
        h = num / jnp.maximum(jnp.abs(den), jnp.exp(-m_t))[..., None]
        m_new = m_t[..., -1]
        w_C = jnp.exp(F[..., -1] + m - m_new)
        k_end = ki * jnp.exp(F[..., -1:] - F + ii - m_new[..., None])[..., None]
        C_new = w_C[..., None, None] * C + jnp.einsum('bhsd,bhsv->bhdv', k_end, vi)
        n_new = w_C[..., None] * n + jnp.sum(k_end, axis=2)
        return (C_new, n_new, m_new), h

    (C_T, n_T, m_T), h = lax.scan(
        step, (C0, n0, m0),
        (split_chunks(q, L), split_chunks(k, L), split_chunks(v, L),
         split_gate_chunks(i_pre, L), split_gate_chunks(log_f, L)))
    return merge_chunks(h), C_T, n_T, m_T

def gla_mixer(x, S0, w_in, w_a2, b_a, g_norm, w_out):
    b, t, _ = x.shape
    q, k, v, r, a_lr = jnp.split(x @ w_in, [QK_W, 2 * QK_W, 2 * QK_W + V_W, 2 * QK_W + 2 * V_W], axis=-1)
    log_a = jax.nn.log_sigmoid((a_lr @ w_a2 + b_a).astype(F32)) / GLA_TAU
    q = q.astype(F32).reshape(b, t, GLA_HEADS, GLA_DK)
    k = k.astype(F32).reshape(b, t, GLA_HEADS, GLA_DK) * GLA_DK ** -0.5
    v = v.astype(F32).reshape(b, t, GLA_HEADS, GLA_DV)
    o, S_T = gla_recurrence(q, k, v, log_a.reshape(b, t, GLA_HEADS, GLA_DK), S0.astype(F32))
    o = rms_norm(o, g_norm).reshape(b, t, V_W).astype(x.dtype)
    y = (jax.nn.silu(r) * o) @ w_out
    return y, S_T.astype(S0.dtype)

def mlstm_mixer(x, C0, n0, m0, w_in, b_gate, g_norm, w_out):
    b, t, _ = x.shape
    q, k, v, o_pre, g_pre = jnp.split(x @ w_in, [QK_W, 2 * QK_W, 2 * QK_W + V_W, 2 * QK_W + 2 * V_W], axis=-1)
    g = GATE_CAP * jnp.tanh((g_pre + b_gate).astype(F32) / GATE_CAP)
    i_pre = g[..., :MLSTM_HEADS]
    log_f = jax.nn.log_sigmoid(g[..., MLSTM_HEADS:])
    q = q.astype(F32).reshape(b, t, MLSTM_HEADS, MLSTM_DK)
    k = k.astype(F32).reshape(b, t, MLSTM_HEADS, MLSTM_DK) * MLSTM_DK ** -0.5
    v = v.astype(F32).reshape(b, t, MLSTM_HEADS, MLSTM_DV)
    h, C_T, n_T, m_T = mlstm_recurrence(q, k, v, i_pre, log_f, C0.astype(F32), n0.astype(F32), m0.astype(F32))
    h = rms_norm(h, g_norm).reshape(b, t, V_W).astype(x.dtype)
    y = (jax.nn.sigmoid(o_pre) * h) @ w_out
    return y, C_T.astype(C0.dtype), n_T.astype(n0.dtype), m_T.astype(m0.dtype)

def swiglu(x, w_gu, w_down):
    g, u = jnp.split(x @ w_gu, 2, axis=-1)
    return (jax.nn.silu(g) * u) @ w_down

def moe_swiglu(x, w_router, b_router, w_gu, w_down):
    probs = jax.nn.softmax((x @ w_router + b_router).astype(F32), axis=-1)
    top_p, top_i = lax.top_k(probs, TOP_K)
    top_p = top_p / jnp.sum(top_p, axis=-1, keepdims=True)
    gates = jnp.sum(jax.nn.one_hot(top_i, N_EXPERTS, dtype=F32) * top_p[..., None], axis=-2)
    y = jnp.zeros_like(x)
    for e in range(N_EXPERTS):
        y = y + (gates[..., e:e + 1] * swiglu(x, w_gu[e], w_down[e]).astype(F32)).astype(x.dtype)
    return y

def trunk(x, gla_S, m_C, m_n, m_m, weights):
    (norm_mix, norm_ffn, norm_final,
     gla_w_in, gla_w_a2, gla_b_a, gla_g_norm, gla_w_out,
     mlstm_w_in, mlstm_b_gate, mlstm_g_norm, mlstm_w_out,
     ffn_w_gu, ffn_w_down,
     moe_w_router, moe_b_router, moe_w_gu, moe_w_down) = weights
    new_S, new_C, new_n, new_m = [], [], [], []
    for i in range(DEPTH):
        j = i // N_MIXERS
        h = rms_norm(x, norm_mix[i])
        if i % N_MIXERS == 0:
            y, S = gla_mixer(h, gla_S[j], gla_w_in[j], gla_w_a2[j], gla_b_a[j], gla_g_norm[j], gla_w_out[j])
            new_S.append(S)
        else:
            y, C, n, m = mlstm_mixer(h, m_C[j], m_n[j], m_m[j], mlstm_w_in[j], mlstm_b_gate[j],
                                     mlstm_g_norm[j], mlstm_w_out[j])
            new_C.append(C)
            new_n.append(n)
            new_m.append(m)
        x = x + y
        h = rms_norm(x, norm_ffn[i])
        jf = i // 2
        if i % 2 == 0:
            x = x + swiglu(h, ffn_w_gu[jf], ffn_w_down[jf])
        else:
            x = x + moe_swiglu(h, moe_w_router[jf], moe_b_router[jf], moe_w_gu[jf], moe_w_down[jf])
    return rms_norm(x, norm_final), jnp.stack(new_S), jnp.stack(new_C), jnp.stack(new_n), jnp.stack(new_m)

def setup_inputs(seed: int = 0) -> dict:
    key = jax.random.key(seed)
    ks = jax.random.split(key, 28)

    def nrm(k, shape, s):
        return jax.random.normal(k, shape, F32) * s

    return {
        'x_prompt': nrm(ks[0], (BATCH, SEQ, D_MODEL), 1.0),
        'x_sample': nrm(ks[1], (DEC_BATCH, DEC_SEQ, D_MODEL), 1.0),
        'state_gla_S': nrm(ks[2], (N_GLA_LAYERS, DEC_BATCH, GLA_HEADS, GLA_DK, GLA_DV), 0.1),
        'state_mlstm_C': nrm(ks[3], (N_MLSTM_LAYERS, DEC_BATCH, MLSTM_HEADS, MLSTM_DK, MLSTM_DV), 0.1),
        'state_mlstm_n': nrm(ks[4], (N_MLSTM_LAYERS, DEC_BATCH, MLSTM_HEADS, MLSTM_DK), 0.1),
        'state_mlstm_m': 2.0 + nrm(ks[5], (N_MLSTM_LAYERS, DEC_BATCH, MLSTM_HEADS), 0.5),
        'norm_mix': 1.0 + nrm(ks[6], (DEPTH, D_MODEL), 0.02),
        'norm_ffn': 1.0 + nrm(ks[7], (DEPTH, D_MODEL), 0.02),
        'norm_final': 1.0 + nrm(ks[8], (D_MODEL,), 0.02),
        'gla_w_in': nrm(ks[9], (N_GLA_LAYERS, D_MODEL, GLA_IN), D_MODEL ** -0.5),
        'gla_w_a2': nrm(ks[10], (N_GLA_LAYERS, GLA_RANK, QK_W), GLA_RANK ** -0.5),
        'gla_b_a': nrm(ks[11], (N_GLA_LAYERS, QK_W), 0.1),
        'gla_g_norm': 1.0 + nrm(ks[12], (N_GLA_LAYERS, GLA_HEADS, GLA_DV), 0.02),
        'gla_w_out': nrm(ks[13], (N_GLA_LAYERS, V_W, D_MODEL), V_W ** -0.5),
        'mlstm_w_in': nrm(ks[14], (N_MLSTM_LAYERS, D_MODEL, MLSTM_IN), D_MODEL ** -0.5),
        'mlstm_b_gate': jnp.concatenate(
            [nrm(ks[15], (N_MLSTM_LAYERS, MLSTM_HEADS), 0.1),
             FORGET_BIAS + nrm(ks[16], (N_MLSTM_LAYERS, MLSTM_HEADS), 0.1)], axis=-1),
        'mlstm_g_norm': 1.0 + nrm(ks[17], (N_MLSTM_LAYERS, MLSTM_HEADS, MLSTM_DV), 0.02),
        'mlstm_w_out': nrm(ks[18], (N_MLSTM_LAYERS, V_W, D_MODEL), V_W ** -0.5),
        'ffn_w_gu': nrm(ks[19], (N_DENSE_LAYERS, D_MODEL, 2 * D_FF), D_MODEL ** -0.5),
        'ffn_w_down': nrm(ks[20], (N_DENSE_LAYERS, D_FF, D_MODEL), D_FF ** -0.5),
        'moe_w_router': nrm(ks[21], (N_MOE_LAYERS, D_MODEL, N_EXPERTS), D_MODEL ** -0.5),
        'moe_b_router': nrm(ks[22], (N_MOE_LAYERS, N_EXPERTS), 0.01),
        'moe_w_gu': nrm(ks[23], (N_MOE_LAYERS, N_EXPERTS, D_MODEL, 2 * D_FF_EXPERT), D_MODEL ** -0.5),
        'moe_w_down': nrm(ks[24], (N_MOE_LAYERS, N_EXPERTS, D_FF_EXPERT, D_MODEL), D_FF_EXPERT ** -0.5),
    }

def reference(x_prompt, x_sample, state_gla_S, state_mlstm_C, state_mlstm_n, state_mlstm_m,
              norm_mix, norm_ffn, norm_final,
              gla_w_in, gla_w_a2, gla_b_a, gla_g_norm, gla_w_out,
              mlstm_w_in, mlstm_b_gate, mlstm_g_norm, mlstm_w_out,
              ffn_w_gu, ffn_w_down,
              moe_w_router, moe_b_router, moe_w_gu, moe_w_down):
    weights = (norm_mix, norm_ffn, norm_final,
               gla_w_in, gla_w_a2, gla_b_a, gla_g_norm, gla_w_out,
               mlstm_w_in, mlstm_b_gate, mlstm_g_norm, mlstm_w_out,
               ffn_w_gu, ffn_w_down,
               moe_w_router, moe_b_router, moe_w_gu, moe_w_down)
    b = x_prompt.shape[0]
    z_S = jnp.zeros((N_GLA_LAYERS, b, GLA_HEADS, GLA_DK, GLA_DV), state_gla_S.dtype)
    z_C = jnp.zeros((N_MLSTM_LAYERS, b, MLSTM_HEADS, MLSTM_DK, MLSTM_DV), state_mlstm_C.dtype)
    z_n = jnp.zeros((N_MLSTM_LAYERS, b, MLSTM_HEADS, MLSTM_DK), state_mlstm_n.dtype)
    z_m = jnp.zeros((N_MLSTM_LAYERS, b, MLSTM_HEADS), state_mlstm_m.dtype)
    y_prompt, S_p, C_p, n_p, m_p = trunk(x_prompt, z_S, z_C, z_n, z_m, weights)
    y_sample, S_s, C_s, n_s, m_s = trunk(x_sample, state_gla_S, state_mlstm_C, state_mlstm_n,
                                         state_mlstm_m, weights)
    return (y_prompt, y_sample, S_p, C_p, n_p, m_p, S_s, C_s, n_s, m_s)


_drawn_inputs = setup_inputs


def setup_inputs(seed=0):
    import zlib

    import numpy as np

    out = dict(_drawn_inputs(seed))
    spreads = {}
    factors = {'norm_final': 8.865, 'mlstm_g_norm': 4.102, 'moe_b_router': 3.401}
    for name, (base, spread) in spreads.items():
        noise = np.random.default_rng([zlib.crc32(name.encode()), seed]).standard_normal(out[name].shape)
        drawn = base * np.exp(spread * noise) if base else spread * noise
        out[name] = jnp.asarray(drawn.astype(out[name].dtype))
    for name, factor in factors.items():
        out[name] = (out[name] * factor).astype(out[name].dtype)
    return out
```

```python
from contextlib import ExitStack

import concourse.bass as bass
from concourse import mybir

F32 = mybir.dt.float32
I32 = mybir.dt.int32
U32 = mybir.dt.uint32
ALU = mybir.AluOpType
ACT = mybir.ActivationFunctionType
AX_X = mybir.AxisListType.X

P = 128
D = 1024
KT = D // P
NP_, NB, NS = 256, 8, 4
NSM = NB * NS
T = NP_ + NSM
L = 64
NC = NP_ // L
TT = 3
TS = [(0, P), (P, P), (NP_, NSM)]
QK = 512
GH, GDV = 4, 256
MH, MDV = 8, 128
RANK = 16
TAU = 16.0
CAPG = 15.0
FF = 2816
NE, FE = 8, 3584
EPS = 1e-6
CAP = 96
MORE = 5
ITEMS = NE + MORE + 1
SLOT = 2048
COLS = SLOT // KT
LO, HI = 7, 7
FFT = FF // P
FBLK = FF // COLS
DG = [(0, 8), (8, 8), (16, 6)]
N_MIX = 2 * QK // COLS + 2 * D // COLS + D // COLS
N_FFN = 2 * FBLK + (D // COLS) * len(DG)
N_STATIC = 2 * N_MIX + N_FFN
STEPS = FE // COLS
PER = 3 * STEPS
BIG = 1024.0


def bank_plan():
    uses, turns = {}, [0] * 8

    def use(name, bank):
        uses[name] = (bank, turns[bank])
        turns[bank] += 1

    use("par", 7)
    for kt in range(KT):
        use(f"x{kt}", kt % 7)
    for layer in range(2):
        l = f"L{layer}"
        use(l + "ss", 3)
        n = 0

        def pj(name):
            nonlocal n
            use(l + name, n % 3)
            n += 1

        if layer == 0:
            pj("lr")
        else:
            pj("gi")
            pj("gf")
        for m in range(4):
            pj(f"q{m}")
        if layer == 0:
            for m in range(4):
                use(f"L0z{m}", 4 + m)
        for m in range(4):
            pj(f"k{m}")
        for s in range(D // COLS):
            for tt in range(TT):
                pj(f"v{s}{tt}")
        if layer == 1:
            use("L1at", 3)
            for j in range(4):
                use(f"L1wb{j}", 4 + j)
        for tt in range(TT):
            use(l + f"kt{tt}", 4 + tt)
        if layer == 0:
            for tt in range(TT):
                use(l + f"sc{tt}", 3)
        else:
            use("L1nu", 7)
            for tt in range(2):
                for hf in range(2):
                    use(f"L1db{tt}{hf}", 3 + hf)
                for hf in range(2):
                    use(f"L1sc{tt}{hf}", 5 + hf)
            use("L1db2", 3)
            use("L1sc2", 5)
        for m in range(8):
            pj(f"r{m}")
        for c in range(NC):
            use(l + f"up{c}a", 6)
            use(l + f"up{c}b", 7)
        for tt in range(2):
            use(l + f"o{tt}a", 4)
            use(l + f"o{tt}b", 5)
        use(l + "o2", 4)
        if layer == 1:
            use("L1den", 3)
        for b in range(NB):
            use(l + f"us{b}a", 6)
            use(l + f"us{b}b", 7)
        use(l + "ns", 5)
        for h in range(GH if layer == 0 else MH):
            use(l + f"nb{h}", h % 3)
        for m in range(8):
            use(l + f"w{m}", 3 + m % 5)
        if layer == 0:
            use("Fss", 3)
            for f in range(FFT):
                base = 0 if (f % 2 == 0) else 4
                use(f"Fg{f}", base)
                use(f"Fu{f}", base + 1)
            for m in range(8):
                use(f"Fw{m}", [2, 3, 6, 7][m % 4])
    use("Mss", 3)
    use("Mlog", 0)
    for kt in range(KT):
        use(f"Mh{kt}", kt)
    for kt in range(KT):
        use(f"Mx{kt}", kt)
    use("Mrank", 1)
    use("Mga0", 7)
    use("Mga1", 6)
    return uses, turns


GU, YB, SCB, TPB, GAB = (0, 1), (2, 3), (4, 5), 6, (7, 6)
LOOP_TURNS = {0: STEPS // 2, 1: STEPS // 2, 2: 1, 3: 1, 4: 3, 5: 3, 6: 2, 7: 1}


def trunk_kernel(nc, ins, outs):
    uses, static_turns = bank_plan()
    (y_p, y_s, S_p, C_p, n_p, m_p, S_s, C_s, n_s, m_s) = outs

    with ExitStack() as ctx:
        def sb(name, shape, dt=F32):
            return ctx.enter_context(nc.sbuf_tensor(name, shape, dt))

        def sem(name):
            return ctx.enter_context(nc.semaphore(name))

        ring_lo = sb("ring_lo", [P, LO * SLOT])
        work = sb("work", [P, 24448])
        xT = sb("xT", [P, KT, T])
        hT = sb("hT", [P, KT, T])
        rbc = sb("rbc", [P, 2, T])
        psum = [ctx.enter_context(nc.psum_tensor(f"bank{b}", [P, 512], F32)) for b in range(8)]

        ident = sb("ident", [P, P])
        ones = sb("ones", [P, P])
        before = sb("before", [P, P])
        causal = sb("causal", [P, P])
        causal_s = sb("causal_s", [NSM, NSM])
        batch_of = sb("batch_of", [NSM, NB])
        going = sb("going", [P, T])
        drop = sb("drop", [MH, T])
        head_row = sb("head_row", [MH, MH, P])
        pair_row = sb("pair_row", [MH, 4, P])
        head_col = sb("head_col", [P, MH, MH])
        slot_no = sb("slot_no", [P, CAP])
        expert_no = sb("expert_no", [P, NE])
        cand_e = sb("cand_e", [P, 2, NE])
        cand_skip = sb("cand_skip", [P, 2, NE])
        more_no = sb("more_no", [P, MORE])
        one_col = sb("one_col", [P, 2])

        par_rows = sb("par_rows", [52, P])
        par = sb("par", [P, 52])
        g_final = sb("g_final", [P, D])
        w_lr = sb("w_lr", [P, KT, RANK])
        w_gate = sb("w_gate", [P, KT, 2 * MH])
        w_a2 = sb("w_a2", [RANK, QK])
        w_rt = sb("w_rt", [P, KT, NE])
        b_rt = sb("b_rt", [P, NE])
        b_i = sb("b_i", [MH, 1])
        b_f = sb("b_f", [MH, 1])
        lr_sb = sb("lr_sb", [RANK, T])
        eb = sb("eb", [P, 4, NC + NB])

        rows = sb("rows", [MH, 10, T])
        m_chunk = sb("m_chunk", [MH, 3, NC + NB])
        a_tok = sb("a_tok", [P, TT, 2, MH])
        n_st = sb("n_st", [P, 2, 4])
        n_sm = sb("n_sm", [P, 4, NB])
        n_new = sb("n_new", [P, 4, NB])
        n_inc = sb("n_inc", [P, 4, NC + NB])
        n_cols = sb("n_cols", [P, 2, MH, MH])

        lg = sb("lg", [P, TT, NE])
        pr = sb("pr", [P, TT, NE])
        top_p = sb("top_p", [P, TT, NE])
        top_i = sb("top_i", [P, TT, NE], U32)
        top_f = sb("top_f", [P, TT, NE])
        st = sb("st", [P, 6, TT])
        oh1 = sb("oh1", [P, TT, NE])
        oh2 = sb("oh2", [P, TT, NE])
        gates = sb("gates", [P, TT, NE])
        chosen = sb("chosen", [P, TT, NE])
        place = sb("place", [P, TT, NE])
        count = sb("count", [P, NE])
        flag = sb("flag", [P, 2, NE])
        order = sb("order", [P, 2, NE])
        pick = sb("pick", [P, MORE, 2 * NE])
        picked = sb("picked", [P, MORE, 2 * NE])
        cand_v = sb("cand_v", [P, 2, NE])
        tab_pos = sb("tab_pos", [P, ITEMS * TT])
        tab_gate = sb("tab_gate", [P, ITEMS * TT])
        tab_f = sb("tab_f", [P, 16])
        tab_i = sb("tab_i", [P, 16], I32)

        def area(at, *dims, rows_=P):
            n = 1
            for d in dims:
                n *= d
            v = work[0:rows_, at:at + n]
            if len(dims) == 2:
                v = v.rearrange("p (a b) -> p a b", a=dims[0])
            if len(dims) == 3:
                v = v.rearrange("p (a b c) -> p a b c", a=dims[0], b=dims[1])
            return v

        xtok = area(9216, TT, D)
        q0 = area(0, 4, T)
        k0 = area(1152, 4, T)
        cum = area(2304, 4, T)
        kend = area(3456, 4, T)
        t1 = area(4608, 4, T)
        t2 = area(5760, 4, T)
        o0 = area(4608, 8, T)
        sq0 = area(2304, 8, T)
        gate_r = area(6912, 8, T)
        v_tok = area(9216, TT, D)
        kz = area(12288, NC + 1, QK)
        P0 = area(14848, 2, GH, P)
        P0s = area(14848 + 1024, GH, NSM, rows_=NSM)
        S0 = area(16000, 2, GH, GDV)
        Ss = area(18048, 3, GH, GDV)
        kb = area(21120, 2, QK, rows_=NSM)
        qz = area(0, MH, T)
        qwz = area(2304, MH, T)
        k1 = area(4608, 4, T)
        dmp = area(5760, MH, P)
        P1 = area(14848, 2, MH, P)
        P1s = area(14848 + 2048, MH, NSM, rows_=NSM)
        C1 = area(17152, 2, 4, MDV)
        Cs = area(18176, 3, 4, MDV)
        qn = area(19712, MH, NSM)
        num = area(22144, MH, T)
        sq1 = area(0, MH, T)
        ffa = area(0, FFT, T)
        ffg = area(6336, 2, T)
        h_tok = area(14336, TT, D)
        x_acc = area(17408, TT, D)
        xg = area(20480, KT, CAP)
        act = area(21248, 2, 2, CAP)
        sg = area(21632, 2, 2 * CAP)
        ye = area(22016, D, rows_=CAP)
        selT = area(23040, TT * P, rows_=CAP)
        sel = area(23424, TT, CAP)
        selg = area(23712, TT, CAP)

        const_ready = sem("const_ready")
        small_loaded = sem("small_loaded")
        x_loaded = sem("x_loaded")
        kz_zero = sem("kz_zero")
        qz_zero = sem("qz_zero")
        slot_loaded = [sem(f"slot_loaded{s}") for s in range(LO + HI)]
        part_used = sem("part_used")
        bank_full = [sem(f"bank_full{b}") for b in range(8)]
        bank_free = [sem(f"bank_free{b}") for b in range(8)]
        v_chain = sem("v_chain")
        a_chain = sem("a_chain")
        sq_ready = sem("sq_ready")
        inv_ready = sem("inv_ready")
        h_ready = sem("h_ready")
        abs_ready = sem("abs_ready")
        ln_ready = sem("ln_ready")
        cum_ready = sem("cum_ready")
        dec_ready = sem("dec_ready")
        qg_ready = sem("qg_ready")
        kend_ready = sem("kend_ready")
        S_loaded = [sem(f"S_loaded{i}") for i in range(3)]
        S_stored = [sem(f"S_stored{i}") for i in range(3)]
        kb_ready = sem("kb_ready")
        osq_ready = sem("osq_ready")
        mean_ready = sem("mean_ready")
        rowx_ready = sem("rowx_ready")
        f_ready = sem("f_ready")
        gated_ready = sem("gated_ready")
        tanh_ready = sem("tanh_ready")
        fabs_ready = sem("fabs_ready")
        fln_ready = sem("fln_ready")
        mexpo_ready = sem("mexpo_ready")
        mexp_ready = sem("mexp_ready")
        q_half = sem("q_half")
        dmp_ready = sem("dmp_ready")
        dexp_ready = sem("dexp_ready")
        qw_ready = sem("qw_ready")
        norm_ready = sem("norm_ready")
        n_new_ready = sem("n_new_ready")
        prompt_S_stored = sem("prompt_S_stored")
        prompt_C_stored = sem("prompt_C_stored")
        small_stored = sem("small_stored")
        pad_zero = sem("pad_zero")
        tok_cleared = sem("tok_cleared")
        logit_ready = sem("logit_ready")
        prob_ready = sem("prob_ready")
        chosen_ready = sem("chosen_ready")
        table_ready = sem("table_ready")
        sel_ready = sem("sel_ready")
        selg_ready = sem("selg_ready")
        silu_ready = sem("silu_ready")
        fsq_ready = sem("fsq_ready")
        fmean_ready = sem("fmean_ready")
        finv_ready = sem("finv_ready")
        out_ready = sem("out_ready")
        out_stored = sem("out_stored")

        N_CONST = 36
        N_SMALL = 16 * 22
        S_LOADS = [3, 3, 2]

        def slot(i):
            s = i % LO
            return ring_lo[:, s * SLOT:(s + 1) * SLOT], s

        def expert_slot(j):
            p = j % (LO + HI)
            if p < LO:
                s = (N_STATIC + p) % LO
                return ring_lo[:, s * SLOT:(s + 1) * SLOT], s
            return work[:, (p - LO) * SLOT:(p - LO + 1) * SLOT], p

        def loads_before(s):
            return len(range(s, N_STATIC, LO)) if s < LO else 0

        def full(name):
            b, k = uses[name]
            return bank_full[b], k + 1

        def copied(name):
            b, k = uses[name]
            return bank_free[b], k + 1

        def loop_full(b, k, i):
            return bank_full[b], i * LOOP_TURNS[b] + (static_turns[b] + k + 1)

        def loop_before(b, k, i):
            return bank_free[b], i * LOOP_TURNS[b] + (static_turns[b] + k)

        def mixer_loads(l, w_in, w_out):
            v = w_in[0].rearrange("(t p) n -> p t n", p=P)
            last = [f"{l}{w}{m}" for w in "qk" for m in (1, 3)] + [f"{l}v{s}2" for s in range(4)] \
                + [f"{l}r{m}" for m in (1, 3, 5, 7)]
            for c, name in enumerate(last):
                yield v[:, :, c * COLS:(c + 1) * COLS], full(name)
            v = w_out[0].rearrange("(t p) n -> p t n", p=P)
            for c in range(D // COLS):
                yield v[:, :, c * COLS:(c + 1) * COLS], full(f"{l}w{2 * c + 1}")

        def ffn_loads():
            v = ins["ffn_w_gu"][0].rearrange("(t p) n -> p t n", p=P)
            for c in range(FBLK):
                for o in (0, FF):
                    yield v[:, :, o + c * COLS:o + (c + 1) * COLS], full(f"Fu{2 * c + 1}")
            v = ins["ffn_w_down"][0].rearrange("(t p) n -> p t n", p=P)
            for c in range(D // COLS):
                for g, (f, k) in enumerate(DG):
                    yield v[:, f:f + k, c * COLS:(c + 1) * COLS], \
                        (part_used, 2 * c + g + 1) if g < 2 else full(f"Fw{2 * c + 1}")

        static_loads = [*mixer_loads("L0", ins["gla_w_in"], ins["gla_w_out"]), *ffn_loads(),
                        *mixer_loads("L1", ins["mlstm_w_in"], ins["mlstm_w_out"])]
        assert len(static_loads) == N_STATIC
        FF_PARTS = 2 * (D // COLS)

        expert_order = [("g", 0), ("u", 0)]
        for j in range(1, STEPS):
            expert_order += [("g", j), ("u", j), ("d", j - 1)]
        expert_order.append(("d", STEPS - 1))
        expert_at = {x: n for n, x in enumerate(expert_order)}

        def expert_used(j, i):
            kind, step = expert_order[j]
            if kind != "d":
                return loop_full(GU[step % 2], step // 2, i)
            if step == STEPS - 1:
                return loop_full(YB[1], 0, i)
            return part_used, i * (STEPS - 1) + (FF_PARTS + step + 1)

        def by_half(ap, a):
            return ap.rearrange("(j a) k v -> a k j v", a=2)[a]

        block = ctx.enter_context(nc.Block())

        @block.sync
        def _(sp):
            for i, (src, _) in enumerate(static_loads):
                dst, s = slot(i)
                if i >= LO:
                    sp.wait_ge(*static_loads[i - LO][1])
                k, n = src.shape[1], src.shape[2]
                sp.dma_start(dst[:, 0:k * n].rearrange("p (k n) -> p k n", k=k), src).then_inc(slot_loaded[s], 16)

            w_gu, w_dn = ins["moe_w_gu"][0], ins["moe_w_down"][0]

            def load(e, j):
                kind, step = expert_order[j]
                dst, s = expert_slot(j)
                if kind == "d":
                    src = w_dn[bass.ds(e, 1), step * COLS:(step + 1) * COLS, :].rearrange("e (t p) n -> p (e t) n", p=P)
                    out = dst.rearrange("p (k n) -> p k n", k=2)
                else:
                    c = step * COLS + (FE if kind == "u" else 0)
                    src = w_gu[bass.ds(e, 1), :, c:c + COLS].rearrange("e (t p) n -> p (e t) n", p=P)
                    out = dst.rearrange("p (k n) -> p k n", k=KT)
                sp.dma_start(out, src).then_inc(slot_loaded[s], 16)

            ring = LO + HI
            for j in range(PER):
                if j < LO:
                    sp.wait_ge(*static_loads[N_STATIC + j - LO][1])
                elif j < ring:
                    sp.wait_ge(*full("L1w7"))
                else:
                    sp.wait_ge(*expert_used(j - ring, 0))
                load(0, j)

            def load_pass(i, e):
                for j in range(PER):
                    if j < ring:
                        sp.wait_ge(*expert_used(j + PER - ring, i - 1))
                    else:
                        sp.wait_ge(*expert_used(j - ring, i))
                    load(e, j)

            with sp.Fori(1, NE - 1) as e:
                load_pass(e, e)
            sp.wait_ge(table_ready, 1)
            n_items = sp.value_load(tab_i[0:1, 15:16], min_val=NE, max_val=NE + MORE)
            with sp.Fori(NE - 1, n_items) as i:
                e = sp.value_load(tab_i[0:1, bass.ds(i, 1)], min_val=0, max_val=NE - 1)
                load_pass(i, e)

        @block.gpsimd
        def _(gp):
            made = [0]

            def c(ins_):
                made[0] += 1
                ins_.then_inc(const_ready, 1)
                gp.wait_ge(const_ready, made[0])

            def keep(t, op, pattern, mult, base=0, fill=0.0):
                c(gp.affine_select(out=t, in_=t, compare_op=op, fill=fill, base=base, pattern=pattern,
                                   channel_multiplier=mult))

            c(gp.memset(ident[:, :], 0.0))
            keep(ident[:, :], ALU.not_equal, [[-1, P]], 1, fill=1.0)
            c(gp.memset(ones[:, :], 1.0))
            c(gp.memset(one_col[:, 0:1], 1.0))
            c(gp.memset(one_col[:, 1:2], 0.0))
            c(gp.memset(before[:, :], 1.0))
            keep(before[:, :], ALU.is_gt, [[1, P]], -1)
            c(gp.memset(causal[:, :], 1.0))
            keep(causal[:, :], ALU.is_ge, [[1, P]], -1)
            keep(causal[:, :].rearrange("p (c t) -> p c t", c=2), ALU.is_ge, [[-L, 2], [0, L]], 1)
            c(gp.memset(causal_s[:, :], 1.0))
            keep(causal_s[:, :], ALU.is_ge, [[1, NSM]], -1)
            keep(causal_s[:, :].rearrange("p (c t) -> p c t", c=NB), ALU.is_ge, [[-NS, NB], [0, NS]], 1)
            c(gp.memset(batch_of[:, :], 1.0))
            keep(batch_of[:, :], ALU.is_ge, [[-NS, NB]], 1)
            keep(batch_of[:, :], ALU.is_ge, [[NS, NB]], -1, base=NS - 1)
            c(gp.memset(going[:, :], 1.0))
            c(gp.memset(going[:, 0:NP_:L], 0.0))
            c(gp.memset(going[:, NP_:T:NS], 0.0))
            c(gp.memset(drop[:, :], 0.0))
            c(gp.memset(drop[:, 0:NP_:L], -3e38))
            c(gp.memset(drop[:, NP_:T:NS], -3e38))
            c(gp.memset(head_row[:, :, :], 0.0))
            keep(head_row[:, :, :], ALU.not_equal, [[1, MH], [0, P]], -1, fill=1.0)
            c(gp.memset(pair_row[:, :, :], 0.0))
            keep(pair_row[:, :, :].rearrange("p j (a m) -> p j a m", a=2), ALU.not_equal, [[2, 4], [1, 2], [0, 64]], -1, fill=1.0)
            c(gp.memset(head_col[:, :, :], 0.0))
            keep(head_col[:, :, :], ALU.not_equal, [[1, MH], [-1, MH]], 0, fill=1.0)
            small = {"allow_small_or_imprecise_dtypes": True}
            c(gp.iota(slot_no[:, :], [[1, CAP]], 0, 0, **small))
            c(gp.iota(expert_no[:, :], [[1, NE]], 0, 0, **small))
            c(gp.iota(cand_e[:, :, :], [[0, 2], [1, NE]], 0, 0, **small))
            c(gp.iota(cand_skip[:, :, :], [[CAP, 2], [0, NE]], CAP, 0, **small))
            c(gp.iota(more_no[:, :], [[1, MORE]], 1, 0, **small))
            c(gp.memset(tab_pos[:, :], -BIG))
            c(gp.memset(tab_gate[:, :], 0.0))
            c(gp.memset(st[:, :, :], 1.0))
            assert made[0] == N_CONST, made[0]

            def load_S(b):
                gp.dma_start(Ss[:, b % 3], ins["state_gla_S"][0, b].rearrange("h k v -> k h v")).then_inc(S_loaded[b % 3], 16)

            for b in range(3):
                load_S(b)
            gp.wait_ge(x_loaded, 48)
            gp.memset(kz[:, :, :], 0.0).then_inc(kz_zero, 1)
            gp.wait_ge(*copied(f"L0up{NC - 1}a"))
            gp.wait_ge(*copied(f"L0up{NC - 1}b"))
            gp.dma_start(S_p[0, 0].rearrange("h k v -> k h v"), S0[:, 0]).then_inc(prompt_S_stored, 16)
            for b in range(NB):
                gp.wait_ge(*copied(f"L0us{b}a"))
                gp.wait_ge(*copied(f"L0us{b}b"))
                gp.dma_start(S_s[0, b].rearrange("h k v -> k h v"), Ss[:, b % 3]).then_inc(S_stored[b % 3], 16)
                if b + 3 < NB:
                    gp.wait_ge(S_stored[b % 3], 16 * (b // 3 + 1))
                    load_S(b + 3)
            for i in range(3):
                gp.wait_ge(S_stored[i], 16 * S_LOADS[i])
            gp.wait_ge(prompt_S_stored, 16)

            def load_C(b):
                for a in range(2):
                    gp.dma_start(Cs[64 * a:64 * a + 64, b % 3], by_half(ins["state_mlstm_C"][0, b], a))\
                        .then_inc(S_loaded[b % 3], 16)

            for b in range(3):
                load_C(b)
            gp.wait_ge(*full("Fw7"))
            gp.memset(area(0, 2 * MH * T), 0.0).then_inc(qz_zero, 1)
            gp.wait_ge(*copied(f"L1up{NC - 1}a"))
            gp.wait_ge(*copied(f"L1up{NC - 1}b"))
            for a in range(2):
                gp.dma_start(by_half(C_p[0, 0], a), C1[64 * a:64 * a + 64, 0]).then_inc(prompt_C_stored, 16)
            for b in range(NB):
                gp.wait_ge(*copied(f"L1us{b}a"))
                gp.wait_ge(*copied(f"L1us{b}b"))
                for a in range(2):
                    gp.dma_start(by_half(C_s[0, b], a), Cs[64 * a:64 * a + 64, b % 3]).then_inc(S_stored[b % 3], 16)
                if b + 3 < NB:
                    gp.wait_ge(S_stored[b % 3], 16 * (S_LOADS[b % 3] + 2 * (b // 3) + 2))
                    load_C(b + 3)
            gp.wait_ge(norm_ready, NC)
            for a in range(2):
                gp.dma_start(n_p[0, 0].rearrange("(j a) k -> a k j", a=2)[a], n_st[64 * a:64 * a + 64, 0], allow_slow_non_contiguous=True).then_inc(small_stored, 16)
            gp.wait_ge(n_new_ready, 1)
            for a in range(2):
                for j in range(4):
                    gp.dma_start(n_s[0].rearrange("b (j a) k -> a j k b", a=2)[a, j], n_new[64 * a:64 * a + 64, j],
                                 allow_slow_non_contiguous=True).then_inc(small_stored, 16)
            gp.dma_start(m_s[0].rearrange("b h -> h b"), m_chunk[:, 1, NC:NC + NB], allow_slow_non_contiguous=True).then_inc(small_stored, 16)
            gp.dma_start(m_p[0, 0].rearrange("(h a) -> h a", a=1), m_chunk[:, 1, NC - 1:NC], allow_slow_non_contiguous=True).then_inc(small_stored, 16)
            gp.wait_ge(small_stored, 16 * 12)
            gp.wait_ge(prompt_C_stored, 32)
            for i in range(3):
                gp.wait_ge(S_stored[i], 16 * 3 * S_LOADS[i])

        @block.tensor
        def _(pe):
            taken = [0]

            def begin(name):
                b, k = uses[name]
                if k:
                    pe.wait_ge(bank_free[b], k)
                return psum[b]

            def end(mm, name):
                mm.then_inc(bank_full[uses[name][0]], 1)

            def weights():
                i = taken[0]
                taken[0] += 1
                s, n = slot(i)
                pe.wait_ge(slot_loaded[n], 16 * (i // LO + 1))
                return s

            pe.wait_ge(const_ready, N_CONST)
            pe.wait_ge(x_loaded, 48)
            for kt in range(KT):
                bk = begin(f"x{kt}")
                for tt, (t0, n) in enumerate(TS):
                    mm = pe.transpose(bk[:, t0:t0 + n], xtok[0:n, tt, kt * P:(kt + 1) * P], ident[0:n, 0:n])
                end(mm, f"x{kt}")
            pe.wait_ge(small_loaded, N_SMALL)
            bk = begin("par")
            end(pe.transpose(bk[:, 0:52], par_rows[:, :], ident[0:52, 0:52]), "par")

            def norm(i, name):
                bk = begin(name)
                for kt in range(KT):
                    pe.wait_ge(sq_ready, KT * i + kt + 1)
                    mm = pe.matmul(bk[:, 0:T], ones[:, :], hT[:, kt, :], start=(kt == 0), stop=(kt == KT - 1))
                end(mm, name)
                pe.wait_ge(h_ready, KT * (i + 1))

            def rows_of(bk, w, src, c, n, m):
                for kt in range(n):
                    mm = pe.matmul(bk[0:m, 0:T], w[:, kt, c:c + m], src[:, kt, :], start=(kt == 0), stop=(kt == n - 1))
                return mm

            def tiles(names, src, n=KT):
                w = weights().rearrange("p (k n) -> p k n", k=n)
                for m, name in enumerate(names):
                    bk = begin(name)
                    end(rows_of(bk, w, src, m * P, n, P), name)

            def mixer_qk(l, which):
                for m in range(0, 4, 2):
                    tiles([f"{l}{which}{m}", f"{l}{which}{m + 1}"], hT)

            def values(l):
                for s in range(D // COLS):
                    w = weights().rearrange("p (k n) -> p k n", k=KT)
                    for tt, (t0, n) in enumerate(TS):
                        name = f"{l}v{s}{tt}"
                        bk = begin(name)
                        for kt in range(KT):
                            mm = pe.matmul(bk[0:n, 0:COLS], hT[:, kt, t0:t0 + n], w[:, kt, :],
                                           start=(kt == 0), stop=(kt == KT - 1))
                        end(mm, name)

            def values_ready(l):
                for tt in range(TT):
                    pe.wait_ge(*copied(f"{l}v{D // COLS - 1}{tt}"))

            def r_pair(l, m):
                tiles([f"{l}r{m}", f"{l}r{m + 1}"], hT)

            def out_proj(l, src):
                for m in range(0, 8, 2):
                    tiles([f"{l}w{m}", f"{l}w{m + 1}"], src)

            norm(0, "L0ss")
            bk = begin("L0lr")
            end(rows_of(bk, w_lr, hT, 0, KT, RANK), "L0lr")
            mixer_qk("L0", "q")
            pe.wait_ge(*copied("L0lr"))
            for m in range(4):
                bk = begin(f"L0z{m}")
                end(pe.matmul(bk[:, 0:T], w_a2[:, m * P:(m + 1) * P], lr_sb[:, :], start=True, stop=True), f"L0z{m}")
            mixer_qk("L0", "k")
            values("L0")

            pe.wait_ge(kend_ready, 1)
            for tt, (t0, n) in enumerate(TS):
                bk = begin(f"L0kt{tt}")
                for h in range(GH):
                    mm = pe.transpose(bk[0:n, h * P:(h + 1) * P], kend[:, h, t0:t0 + n], ident[:, :])
                end(mm, f"L0kt{tt}")
            pe.wait_ge(qg_ready, 2)
            for tt, (t0, n) in enumerate(TS):
                if tt == 1:
                    r_pair("L0", 0)
                bk = begin(f"L0sc{tt}")
                for h in range(GH):
                    mm = pe.matmul(bk[0:n, h * n:(h + 1) * n], k0[:, h, t0:t0 + n], q0[:, h, t0:t0 + n], start=True, stop=True)
                end(mm, f"L0sc{tt}")

            def update(l, c):
                for half, x in enumerate("ab"):
                    name = f"{l}up{c}{x}"
                    bk = begin(name)
                    for h in range(2):
                        g = 2 * half + h
                        mm = pe.matmul(bk[:, h * 256:(h + 1) * 256], kz[:, c, g * P:(g + 1) * P],
                                       v_tok[:, c // 2, g * 256:(g + 1) * 256], start=True, stop=True)
                    end(mm, name)

            def update_sample(l, b, n_before):
                pe.wait_ge(kb_ready, n_before + b + 1)
                for half, x in enumerate("ab"):
                    name = f"{l}us{b}{x}"
                    bk = begin(name)
                    for h in range(2):
                        g = 2 * half + h
                        mm = pe.matmul(bk[:, h * 256:(h + 1) * 256], kb[:, b % 2, g * P:(g + 1) * P],
                                       v_tok[0:NSM, 2, g * 256:(g + 1) * 256], start=True, stop=True)
                    end(mm, name)

            def own_part(tt, n, scores, names):
                per = 8 // len(names)
                for half, name in enumerate(names):
                    bk = begin(name)
                    for m in range(per):
                        g = per * half + m
                        pe.matmul(bk[:, m * n:(m + 1) * n], v_tok[0:n, tt, g * P:(g + 1) * P], scores(g),
                                  start=(m == 0), stop=False, skip_group_check=True)

            def state_part(l, c, state, query, done):
                pe.wait_ge(*copied(f"{l}up{c - 1}a"))
                pe.wait_ge(*copied(f"{l}up{c - 1}b"))
                for half, x in enumerate("ab"):
                    name = f"{l}o{c // 2}{x}"
                    bk = psum[uses[name][0]]
                    for m in range(4):
                        g = 4 * half + m
                        o = m * P + (c % 2) * L
                        mm = pe.matmul(bk[:, o:o + L], state(g), query(g), start=False, stop=True, skip_group_check=True)
                    if done:
                        end(mm, name)

            def inter0(c, done):
                state_part("L0", c, lambda g: S0[:, c % 2, g // 2, (g % 2) * P:(g % 2 + 1) * P],
                           lambda g: q0[:, g // 2, c * L:(c + 1) * L], done)

            for tt in range(TT):
                pe.wait_ge(*copied(f"L0kt{tt}"))
            values_ready("L0")
            update("L0", 0)
            r_pair("L0", 2)
            update("L0", 1)
            pe.wait_ge(*copied("L0sc0"))
            own_part(0, P, lambda g: P0[:, 0, g // 2, :], ["L0o0a", "L0o0b"])
            inter0(1, True)
            update("L0", 2)
            r_pair("L0", 4)
            pe.wait_ge(*copied("L0sc1"))
            own_part(1, P, lambda g: P0[:, 1, g // 2, :], ["L0o1a", "L0o1b"])
            inter0(2, False)
            update("L0", 3)
            r_pair("L0", 6)
            inter0(3, True)
            pe.wait_ge(*copied("L0sc2"))
            own_part(2, NSM, lambda g: P0s[:, g // 2, :], ["L0o2"])
            for b in range(NB):
                pe.wait_ge(S_loaded[b % 3], 16 * (b // 3 + 1))
                bk = psum[uses["L0o2"][0]]
                for g in range(8):
                    o = g * NSM + b * NS
                    mm = pe.matmul(bk[:, o:o + NS], Ss[:, b % 3, g // 2, (g % 2) * P:(g % 2 + 1) * P],
                                   q0[:, g // 2, NP_ + b * NS:NP_ + (b + 1) * NS], start=False, stop=True, skip_group_check=True)
                if b == NB - 1:
                    end(mm, "L0o2")
                update_sample("L0", b, 0)

            bk = begin("L0ns")
            for g in range(8):
                pe.wait_ge(osq_ready, g // 2 + 1)
                mm = pe.matmul(bk[0:MH, 0:T], head_col[:, g // 2, :], sq0[:, g, :], start=(g == 0), stop=(g == 7))
            end(mm, "L0ns")
            pe.wait_ge(f_ready, 1)
            for h in range(GH):
                bk = begin(f"L0nb{h}")
                end(pe.matmul(bk[:, 0:T], head_row[:, h, :], rows[:, 0, :], start=True, stop=True), f"L0nb{h}")
            pe.wait_ge(gated_ready, 8)
            out_proj("L0", o0)

            norm(1, "Fss")
            for c in range(FBLK):
                wg = weights().rearrange("p (k n) -> p k n", k=KT)
                wu = weights().rearrange("p (k n) -> p k n", k=KT)
                for m in range(2):
                    f = 2 * c + m
                    for w, name in ((wg, f"Fg{f}"), (wu, f"Fu{f}")):
                        bk = begin(name)
                        end(rows_of(bk, w, hT, m * P, KT, P), name)
            pe.wait_ge(*copied(f"Fu{FFT - 2}"))
            pe.wait_ge(*copied(f"Fu{FFT - 1}"))
            for c in range(D // COLS):
                banks = [begin(f"Fw{2 * c + m}") for m in range(2)]
                for g, (f0, k) in enumerate(DG):
                    w = weights()[:, 0:k * COLS].rearrange("p (k n) -> p k n", k=k)
                    for m in range(2):
                        for f in range(k):
                            mm = pe.matmul(banks[m][:, 0:T], w[:, f, m * P:(m + 1) * P], ffa[:, f0 + f, :],
                                           start=(f0 + f == 0), stop=(f0 + f == FFT - 1))
                        if g == 2:
                            end(mm, f"Fw{2 * c + m}")
                    if g < 2:
                        mm.then_inc(part_used, 1)

            norm(2, "L1ss")
            for a, name in enumerate(("L1gi", "L1gf")):
                bk = begin(name)
                end(rows_of(bk, w_gate, hT, MH * a, KT, MH), name)
            mixer_qk("L1", "q")
            mixer_qk("L1", "k")
            values("L1")

            pe.wait_ge(mexp_ready, 1)
            bk = begin("L1at")
            for tt, (t0, n) in enumerate(TS):
                for a, r in enumerate((2, 7)):
                    c = (2 * tt + a) * MH
                    mm = pe.transpose(bk[0:n, c:c + MH], rows[:, r, t0:t0 + n], ident[0:MH, 0:MH])
            end(mm, "L1at")
            for j in range(4):
                bk = begin(f"L1wb{j}")
                end(pe.matmul(bk[:, 0:T], pair_row[:, j, :], rows[:, 5, :], start=True, stop=True), f"L1wb{j}")
            for m in range(4):
                pe.wait_ge(*copied(f"L1k{m}"))
            for tt, (t0, n) in enumerate(TS):
                bk = begin(f"L1kt{tt}")
                for j in range(4):
                    mm = pe.transpose(bk[0:n, j * P:(j + 1) * P], k1[:, j, t0:t0 + n], ident[:, :])
                end(mm, f"L1kt{tt}")

            def decay_and_scores(tt, t0, n, parts, halves):
                per = MH // halves
                for kind in ("db", "sc"):
                    for hf in range(halves):
                        name = f"L1{kind}{tt}{parts[hf]}"
                        bk = begin(name)
                        for h in range(per):
                            g = per * hf + h
                            if kind == "db":
                                mm = pe.matmul(bk[0:n, h * n:(h + 1) * n], head_row[:, g, 0:n], rows[:, 4, t0:t0 + n], start=True, stop=True)
                            else:
                                mm = pe.matmul(bk[0:n, h * n:(h + 1) * n], k1[:, g // 2, t0:t0 + n], qz[:, g, t0:t0 + n], start=True, stop=True)
                        end(mm, name)

            decay_and_scores(0, 0, P, "01", 2)
            r_pair("L1", 0)
            for tt in range(TT):
                pe.wait_ge(*copied(f"L1kt{tt}"))
            bk = begin("L1nu")
            for j in range(4):
                for c in range(NC):
                    pe.matmul(bk[:, j * 12 + c:j * 12 + c + 1], kz[:, c, j * P:(j + 1) * P], ones[:, 0:1], start=True, stop=True)
                mm = pe.matmul(bk[:, j * 12 + NC:(j + 1) * 12], kz[0:NSM, NC, j * P:(j + 1) * P], batch_of[:, :], start=True, stop=True)
            end(mm, "L1nu")
            decay_and_scores(1, P, P, "01", 2)
            r_pair("L1", 2)
            decay_and_scores(2, NP_, NSM, [""], 1)

            den = psum[uses["L1den"][0]]

            def den_own(tt, t0, n, Pm):
                for g in range(MH):
                    pe.matmul(den[0:MH, t0:t0 + n], head_col[0:n, g, :], Pm[:, g, :], start=(tt == 0 and g == 0),
                              stop=False, skip_group_check=True)

            def inter1(c, done):
                pe.wait_ge(norm_ready, c)
                for g in range(MH):
                    pe.matmul(den[0:MH, c * L:(c + 1) * L], n_cols[:, c % 2, g, :], qwz[:, g, c * L:(c + 1) * L],
                              start=False, stop=True, skip_group_check=True)
                state_part("L1", c, lambda g: C1[:, c % 2, g // 2, :], lambda g: qwz[:, g, c * L:(c + 1) * L], done)

            values_ready("L1")
            update("L1", 0)
            update("L1", 1)
            r_pair("L1", 4)
            pe.wait_ge(*copied("L1sc00"))
            pe.wait_ge(*copied("L1sc01"))
            own_part(0, P, lambda g: P1[:, 0, g, :], ["L1o0a", "L1o0b"])
            begin("L1den")
            den_own(0, 0, P, P1[:, 0])
            inter1(1, True)
            update("L1", 2)
            pe.wait_ge(*copied("L1sc10"))
            pe.wait_ge(*copied("L1sc11"))
            own_part(1, P, lambda g: P1[:, 1, g, :], ["L1o1a", "L1o1b"])
            den_own(1, P, P, P1[:, 1])
            inter1(2, False)
            update("L1", 3)
            r_pair("L1", 6)
            inter1(3, True)
            pe.wait_ge(*copied("L1sc2"))
            own_part(2, NSM, lambda g: P1s[:, g, :], ["L1o2"])
            den_own(2, NP_, NSM, P1s)
            pe.wait_ge(norm_ready, NC + 1)
            for g in range(MH):
                mm = pe.matmul(den[0:MH, NP_:T], head_col[:, g, :], qn[:, g, :], start=False, stop=True, skip_group_check=True)
            end(mm, "L1den")
            for b in range(NB):
                pe.wait_ge(S_loaded[b % 3], 16 * (S_LOADS[b % 3] + 2 * (b // 3) + 2))
                bk = psum[uses["L1o2"][0]]
                for g in range(MH):
                    o = g * NSM + b * NS
                    mm = pe.matmul(bk[:, o:o + NS], Cs[:, b % 3, g // 2, :], qwz[:, g, NP_ + b * NS:NP_ + (b + 1) * NS],
                                   start=False, stop=True, skip_group_check=True)
                if b == NB - 1:
                    end(mm, "L1o2")
                update_sample("L1", b, NB)
            bk = begin("L1ns")
            for g in range(MH):
                pe.wait_ge(osq_ready, GH + g + 1)
                mm = pe.matmul(bk[0:MH, 0:T], head_col[:, g, :], sq1[:, g, :], start=(g == 0), stop=(g == 7))
            end(mm, "L1ns")
            pe.wait_ge(f_ready, 2)
            for h in range(MH):
                bk = begin(f"L1nb{h}")
                end(pe.matmul(bk[:, 0:T], head_row[:, h, :], rows[:, 0, :], start=True, stop=True), f"L1nb{h}")
            pe.wait_ge(gated_ready, 16)
            out_proj("L1", num)

            norm(3, "Mss")
            bk = begin("Mlog")
            for tt, (t0, n) in enumerate(TS):
                for kt in range(KT):
                    mm = pe.matmul(bk[0:n, tt * NE:(tt + 1) * NE], hT[:, kt, t0:t0 + n], w_rt[:, kt, :],
                                   start=(kt == 0), stop=(kt == KT - 1))
            end(mm, "Mlog")
            for c, src in (("h", hT), ("x", xT)):
                for kt in range(KT):
                    bk = begin(f"M{c}{kt}")
                    for tt, (t0, n) in enumerate(TS):
                        mm = pe.transpose(bk[0:n, tt * P:(tt + 1) * P], src[:, kt, t0:t0 + n], ident[:, :])
                    end(mm, f"M{c}{kt}")
            pe.wait_ge(chosen_ready, 1)
            bk = begin("Mrank")
            for tt in range(TT):
                for s in range(tt + 1):
                    pe.matmul(bk[:, tt * NE:(tt + 1) * NE], (before if s == tt else ones)[:, :], chosen[:, s, :],
                              start=(s == 0), stop=(s == tt))
            for s in range(TT):
                mm = pe.matmul(bk[:, TT * NE:(TT + 1) * NE], ones[:, :], chosen[:, s, :], start=(s == 0), stop=(s == TT - 1))
            end(mm, "Mrank")

            def gather(bank_of):
                for half in range(2):
                    b = bank_of(half)
                    for m in range(4):
                        kt = 4 * half + m
                        for tt in range(TT):
                            mm = pe.matmul(psum[b][:, m * CAP:(m + 1) * CAP], h_tok[:, tt, kt * P:(kt + 1) * P], sel[:, tt, :],
                                           start=(tt == 0), stop=(tt == TT - 1))
                    mm.then_inc(bank_full[b], 1)

            def first_bank(half):
                begin(f"Mga{half}")
                return uses[f"Mga{half}"][0]

            for kt in range(KT):
                pe.wait_ge(*copied(f"Mh{kt}"))
            pe.wait_ge(sel_ready, 1)
            gather(first_bank)
            pe.wait_ge(table_ready, 1)
            n_items = pe.value_load(tab_i[0:1, 15:16], min_val=NE, max_val=NE + MORE)

            def scatter(i):
                pe.wait_ge(pad_zero, 1)
                pe.wait_ge(*loop_before(YB[0], 0, i))
                pe.wait_ge(*loop_before(YB[1], 0, i))
                pe.wait_ge(*loop_before(GAB[1], 0, i))
                for n in range(6):
                    tt, half = n // 2, n % 2
                    b = SCB[n % 2]
                    pe.wait_ge(*loop_before(b, n // 2, i))
                    pe.matmul(psum[b][:, :], selT[:, tt * P:(tt + 1) * P], ye[:, half * 512:(half + 1) * 512],
                              start=True, stop=True).then_inc(bank_full[b], 1)

            with pe.Fori(0, n_items) as i:
                def expert_weights(kind, step):
                    at = expert_at[kind, step]
                    s, n = expert_slot(at)
                    pe.wait_ge(slot_loaded[n], i * (16 * PER // (LO + HI)) + 16 * (loads_before(n) + at // (LO + HI) + 1))
                    return s.rearrange("p (k n) -> p k n", k=2 if kind == "d" else KT)

                def down(step):
                    w = expert_weights("d", step)
                    b = GU[step % 2]
                    pe.wait_ge(*loop_before(b, step // 2 + 1, i))
                    if step == 0:
                        pe.wait_ge(*loop_before(YB[0], 0, i))
                        pe.wait_ge(*loop_before(YB[1], 0, i))
                    for f in range(2):
                        for half in range(2):
                            mm = pe.matmul(psum[YB[half]][0:CAP, :], act[:, step % 2, f, :], w[:, f, half * 512:(half + 1) * 512],
                                           start=(step == 0 and f == 0), stop=(step == STEPS - 1 and f == 1),
                                           skip_group_check=True)
                            if step == STEPS - 1 and f == 1:
                                mm.then_inc(bank_full[YB[half]], 1)
                    if step < STEPS - 1:
                        mm.then_inc(part_used, 1)

                for step in range(STEPS):
                    wg = expert_weights("g", step)
                    wu = expert_weights("u", step)
                    if step == 0:
                        pe.wait_ge(*loop_before(GAB[0], 0, i))
                        pe.wait_ge(*loop_before(GAB[1], 0, i))
                    b = GU[step % 2]
                    pe.wait_ge(*loop_before(b, step // 2, i))
                    for a, w in enumerate((wg, wu)):
                        for f in range(2):
                            c = (2 * a + f) * CAP
                            for kt in range(KT):
                                mm = pe.matmul(psum[b][:, c:c + CAP], w[:, kt, f * P:(f + 1) * P], xg[:, kt, :],
                                               start=(kt == 0), stop=(kt == KT - 1))
                    mm.then_inc(bank_full[b], 1)
                    if step == 0:
                        scatter(i)
                    else:
                        down(step - 1)
                pe.wait_ge(selg_ready, i + 1)
                pe.wait_ge(*loop_before(TPB, 0, i))
                for tt in range(TT):
                    mm = pe.transpose(psum[TPB][0:CAP, tt * P:(tt + 1) * P], selg[:, tt, :], ident[:, :])
                mm.then_inc(bank_full[TPB], 1)
                pe.wait_ge(sel_ready, i + 2)

                def next_bank(half):
                    pe.wait_ge(*loop_before(GAB[half], half, i))
                    return GAB[half]

                gather(next_bank)
                down(STEPS - 1)
            scatter(n_items)

        @block.scalar
        def _(ac):
            chain = [0]

            def step(ins_):
                chain[0] += 1
                ins_.then_inc(a_chain, 1)
                ac.wait_ge(a_chain, chain[0])

            def take(name):
                b, k = uses[name]
                ac.wait_ge(bank_full[b], k + 1)
                return psum[b]

            def free(ins_, name):
                ins_.then_inc(bank_free[uses[name][0]], 1)

            one, zero = one_col[:, 0:1], one_col[:, 1:2]
            for tt in range(2):
                ac.dma_start(xtok[:, tt, :], ins["x_prompt"][0, tt * P:(tt + 1) * P, :]).then_inc(x_loaded, 16)
            ac.dma_start(xtok[0:NSM, 2, :], ins["x_sample"].rearrange("b t d -> (b t) d")).then_inc(x_loaded, 16)

            def small(dst, src):
                ac.dma_start(dst, src, allow_slow_non_contiguous=True).then_inc(small_loaded, 16)

            small(par_rows[0:16, :], ins["norm_mix"].rearrange("l (t p) -> (l t) p", p=P))
            small(par_rows[16:32, :], ins["norm_ffn"].rearrange("l (t p) -> (l t) p", p=P))
            small(par_rows[32:36, :], ins["gla_b_a"].rearrange("l (t p) -> (l t) p", p=P))
            small(par_rows[36:44, :], ins["gla_g_norm"].rearrange("l h (t p) -> (l h t) p", p=P))
            small(par_rows[44:52, :], ins["mlstm_g_norm"].rearrange("l h p -> (l h) p"))
            small(w_lr[:, :, :], ins["gla_w_in"][0, :, 3072:3088].rearrange("(t p) n -> p t n", p=P))
            small(w_gate[:, :, :], ins["mlstm_w_in"][0, :, 3072:3088].rearrange("(t p) n -> p t n", p=P))
            small(w_a2[:, :], ins["gla_w_a2"][0])
            small(w_rt[:, :, :], ins["moe_w_router"][0].rearrange("(t p) n -> p t n", p=P))
            small(b_rt[:, :], ins["moe_b_router"].broadcast_to([P, NE]))
            small(g_final[:, :], ins["norm_final"].rearrange("(a n) -> a n", a=1).broadcast_to([P, D]))
            small(b_i[:, :], ins["mlstm_b_gate"][0, 0:MH].rearrange("(h a) -> h a", a=1))
            small(b_f[:, :], ins["mlstm_b_gate"][0, MH:2 * MH].rearrange("(h a) -> h a", a=1))
            small(m_chunk[:, 0, NC:NC + NB], ins["state_mlstm_m"][0].rearrange("b h -> h b"))
            for a in range(2):
                for j in range(4):
                    small(n_sm[64 * a:64 * a + 64, j, :], ins["state_mlstm_n"][0].rearrange("b (j a) k -> a j k b", a=2)[a, j])

            def norm(i, name, source, readers):
                if readers:
                    ac.wait_ge(*full(readers))
                for kt in range(KT):
                    ac.wait_ge(*copied(f"{source}{kt}"))
                    ac.activation(hT[:, kt, :], xT[:, kt, :], ACT.Square, bias=zero).then_inc(sq_ready, 1)
                ac.wait_ge(*copied(name))
                step(ac.activation(rbc[:, 1, :], rbc[:, 0, :], ACT.Ln, bias=zero))
                ac.activation(rbc[:, 1, :], rbc[:, 1, :], ACT.Exp, bias=zero, scale=-0.5).then_inc(inv_ready, 1)

            def head_norm(n):
                ac.wait_ge(mean_ready, n)
                step(ac.activation(rows[:, 1, :], rows[:, 0, :], ACT.Ln, bias=zero[0:MH]))
                ac.activation(rows[:, 1, :], rows[:, 1, :], ACT.Exp, bias=zero[0:MH], scale=-0.5).then_inc(rowx_ready, 1)

            def values(l):
                for s in range(D // COLS):
                    for tt, (t0, n) in enumerate(TS):
                        name = f"{l}v{s}{tt}"
                        free(ac.activation(v_tok[0:n, tt, s * COLS:(s + 1) * COLS], take(name)[0:n, 0:COLS], ACT.Copy), name)

            def gate(l, m, func):
                free(ac.activation(gate_r[:, m, :], take(f"{l}r{m}")[:, 0:T], func, bias=zero), f"{l}r{m}")

            def output(l, o, tt):
                if tt < 2:
                    for half, x in enumerate("ab"):
                        name = f"{l}o{tt}{x}"
                        free(ac.activation(o[:, 4 * half:4 * half + 4, tt * P:(tt + 1) * P],
                                           take(name)[:, :].rearrange("p (g t) -> p g t", g=4), ACT.Copy), name)
                else:
                    name = l + "o2"
                    free(ac.activation(o[:, :, NP_:T], take(name)[:, 0:8 * NSM].rearrange("p (g t) -> p g t", g=8), ACT.Copy), name)

            ac.wait_ge(const_ready, N_CONST)
            norm(0, "L0ss", "x", None)
            free(ac.activation(lr_sb[:, :], take("L0lr")[0:RANK, 0:T], ACT.Copy), "L0lr")
            for m in range(4):
                free(ac.activation(q0[:, m, :], take(f"L0q{m}")[:, 0:T], ACT.Copy), f"L0q{m}")
            for h in range(4):
                ac.wait_ge(abs_ready, h + 1)
                step(ac.activation(t2[:, h, :], t2[:, h, :], ACT.Exp, bias=zero, scale=-1.0))
                ac.activation(t2[:, h, :], t2[:, h, :], ACT.Ln, bias=one).then_inc(ln_ready, 1)
            for m in range(4):
                free(ac.activation(k0[:, m, :], take(f"L0k{m}")[:, 0:T], ACT.Copy, scale=float(P) ** -0.5), f"L0k{m}")
            ac.wait_ge(cum_ready, 6)
            ac.activation(t1[:, :, :], cum[:, :, :], ACT.Exp, bias=zero, scale=1 / TAU).then_inc(dec_ready, 1)
            ac.activation(t2[:, :, :], t2[:, :, :], ACT.Exp, bias=zero, scale=1 / TAU).then_inc(dec_ready, 1)
            ac.activation(eb[:, :, 0:NC], cum[:, :, L - 1:NP_:L], ACT.Exp, bias=zero, scale=1 / TAU).then_inc(dec_ready, 1)
            ac.activation(eb[:, :, NC:NC + NB], cum[:, :, NP_ + NS - 1:T:NS], ACT.Exp, bias=zero, scale=1 / TAU).then_inc(dec_ready, 1)
            ac.wait_ge(qg_ready, 1)
            ac.activation(t1[:, :, :], cum[:, :, :], ACT.Exp, bias=zero, scale=-1 / TAU).then_inc(dec_ready, 1)
            values("L0")
            for m in range(4):
                gate("L0", m, ACT.Silu)
            ac.wait_ge(qg_ready, 2)
            output("L0", o0, 0)
            for m in range(4, 8):
                gate("L0", m, ACT.Silu)
            output("L0", o0, 1)
            output("L0", o0, 2)
            ac.wait_ge(*copied("L0o2"))
            ac.wait_ge(*copied("L0o1b"))
            ac.wait_ge(*full("L0sc2"))
            for h in range(GH):
                ac.activation(sq0[:, 2 * h:2 * h + 2, :], o0[:, 2 * h:2 * h + 2, :], ACT.Square, bias=zero).then_inc(osq_ready, 1)
            head_norm(1)

            norm(1, "Fss", "L0w", "L0r7")
            for f in range(FFT):
                if f >= 2:
                    ac.wait_ge(*copied(f"Fu{f - 2}"))
                free(ac.activation(ffg[:, f % 2, :], take(f"Fg{f}")[:, 0:T], ACT.Silu, bias=zero), f"Fg{f}")

            norm(2, "L1ss", "Fw", f"Fu{FFT - 1}")
            ac.wait_ge(*copied("L1gf"))
            for r in range(2):
                ac.activation(rows[:, r, :], rows[:, r, :], ACT.Tanh, bias=zero[0:MH], scale=1 / CAPG).then_inc(tanh_ready, 1)
            ac.wait_ge(qz_zero, 1)

            def q_pair(m):
                bk = take(f"L1q{m}")
                ac.activation(qz[0:64, 2 * m, :], bk[0:64, 0:T], ACT.Copy).then_inc(q_half, 1)
                free(ac.activation(qz[64:128, 2 * m + 1, :], bk[64:128, 0:T], ACT.Copy), f"L1q{m}")

            q_pair(0)
            q_pair(1)
            ac.wait_ge(fabs_ready, 1)
            step(ac.activation(rows[:, 2, :], rows[:, 2, :], ACT.Exp, bias=zero[0:MH], scale=-1.0))
            ac.activation(rows[:, 2, :], rows[:, 2, :], ACT.Ln, bias=one[0:MH]).then_inc(fln_ready, 1)
            q_pair(2)
            q_pair(3)
            for m in range(4):
                free(ac.activation(k1[:, m, :], take(f"L1k{m}")[:, 0:T], ACT.Copy, scale=64.0 ** -0.5), f"L1k{m}")
            ac.wait_ge(mexpo_ready, 1)
            ac.activation(rows[:, 5:8, :], rows[:, 5:8, :], ACT.Exp, bias=zero[0:MH]).then_inc(mexp_ready, 1)
            values("L1")
            for tt, (t0, n) in enumerate(TS):
                ac.wait_ge(dmp_ready, tt + 1)
                v = dmp[0:n, :, 0:n]
                ac.activation(v, v, ACT.Exp, bias=zero[0:n]).then_inc(dexp_ready, 1)
                if tt < 2:
                    for m in (2 * tt, 2 * tt + 1):
                        gate("L1", m, ACT.Sigmoid)
            gate("L1", 4, ACT.Sigmoid)
            gate("L1", 5, ACT.Sigmoid)
            output("L1", num, 0)
            gate("L1", 6, ACT.Sigmoid)
            gate("L1", 7, ACT.Sigmoid)
            output("L1", num, 1)
            output("L1", num, 2)
            ac.wait_ge(*copied("L1o2"))
            ac.wait_ge(*copied("L1o1b"))
            ac.wait_ge(qw_ready, 8)
            for h in range(MH):
                ac.activation(sq1[:, h, :], num[:, h, :], ACT.Square, bias=zero).then_inc(osq_ready, 1)
            head_norm(2)

            norm(3, "Mss", "L1w", "L1r7")
            ac.wait_ge(logit_ready, 1)
            ac.activation(pr[:, :, :], lg[:, :, :], ACT.Exp, bias=zero).then_inc(prob_ready, 1)
            ac.wait_ge(tok_cleared, 1)
            for kt in range(KT):
                bk = take(f"Mh{kt}")
                step(ac.activation(h_tok[:, 0:2, kt * P:(kt + 1) * P], bk[:, 0:2 * P].rearrange("p (a b) -> p a b", a=2), ACT.Copy))
                free(ac.activation(h_tok[0:NSM, 2, kt * P:(kt + 1) * P], bk[0:NSM, 2 * P:3 * P], ACT.Copy), f"Mh{kt}")
            ac.wait_ge(table_ready, 1)
            n_items = ac.value_load(tab_i[0:1, 15:16], min_val=NE, max_val=NE + MORE)
            with ac.Fori(0, n_items) as i:
                for s in range(STEPS):
                    b = GU[s % 2]
                    ac.wait_ge(*loop_full(b, s // 2, i))
                    ac.wait_ge(*loop_before(b, s // 2, i))
                    ac.activation(sg[:, s % 2, :], psum[b][:, 0:2 * CAP], ACT.Silu, bias=zero).then_inc(silu_ready, 1)
                for half in range(2):
                    ac.wait_ge(*loop_full(YB[half], 0, i))
                    ac.activation(ye[:, half * 512:(half + 1) * 512], psum[YB[half]][0:CAP, :], ACT.Copy)\
                        .then_inc(bank_free[YB[half]], 1)

            for b in SCB:
                ac.wait_ge(*loop_before(b, 3, n_items))
            ac.wait_ge(*loop_full(GAB[1], -1, n_items))
            for tt, (t0, n) in enumerate(TS):
                ac.activation(h_tok[0:n, tt, :], x_acc[0:n, tt, :], ACT.Square, bias=zero[0:n],
                              accum_out=st[0:n, 4, tt:tt + 1]).then_inc(fsq_ready, 1)
            ac.wait_ge(fmean_ready, 1)
            step(ac.activation(st[:, 5, :], st[:, 4, :], ACT.Ln, bias=zero))
            ac.activation(st[:, 5, :], st[:, 5, :], ACT.Exp, bias=zero, scale=-0.5).then_inc(finv_ready, 1)
            for tt, (t0, n) in enumerate(TS):
                ac.wait_ge(out_ready, tt + 1)
                dst = y_p[0, t0:t0 + n, :] if tt < 2 else y_s.rearrange("b t d -> (b t) d")
                ac.dma_start(dst, x_acc[0:n, tt, :]).then_inc(out_stored, 16)
            ac.wait_ge(out_stored, 48)

        @block.vector
        def _(ve):
            chain = [0]

            def step(ins_):
                chain[0] += 1
                ins_.then_inc(v_chain, 1)
                ve.wait_ge(v_chain, chain[0])

            def take(name):
                b, k = uses[name]
                ve.wait_ge(bank_full[b], k + 1)
                return psum[b]

            def free(ins_, name):
                ins_.then_inc(bank_free[uses[name][0]], 1)

            def free_step(ins_, name):
                free(ins_, name)
                ve.wait_ge(*copied(name))

            def stt(out, a, s, b, op0, op1):
                return ve.scalar_tensor_tensor(out=out, in0=a, scalar=s, in1=b, op0=op0, op1=op1)

            def polish(x, y, t, last):
                step(stt(t, x, -0.5, y, ALU.mult, ALU.mult))
                step(ve.tensor_tensor(t, t, y, ALU.mult))
                last(stt(y, t, 1.5, y, ALU.add, ALU.mult))

            def norm(i, name):
                free(ve.tensor_scalar(rbc[:, 0, :], take(name)[:, 0:T], 1.0 / D, EPS, ALU.mult, ALU.add), name)
                ve.wait_ge(inv_ready, i + 1)
                polish(rbc[:, 0, :], rbc[:, 1, :], rbc[:, 0, :], step)
                g0 = [0, 16, 8, 24][i]
                for kt in range(KT):
                    stt(hT[:, kt, :], xT[:, kt, :], par[:, g0 + kt:g0 + kt + 1], rbc[:, 1, :], ALU.mult, ALU.mult)\
                        .then_inc(h_ready, 1)

            def residual(prefix):
                for m in range(KT):
                    name = f"{prefix}{m}"
                    free(ve.tensor_tensor(xT[:, m, :], xT[:, m, :], take(name)[:, 0:T], ALU.add), name)

            def over_heads(m, n):
                p = m.shape[0]
                return m.unsqueeze(1).broadcast_to([p, n, m.shape[1]])

            def sample_keys(l, b, n_before):
                if b >= 2:
                    ve.wait_ge(*full(f"{l}us{b - 2}b"))
                ve.tensor_scalar(kb[:, b % 2, :], kz[0:NSM, NC, :], batch_of[:, b:b + 1], None, ALU.mult).then_inc(kb_ready, 1)

            def gated(l, o, heads, tiles_, g0):
                for h in range(heads):
                    bk = take(f"{l}nb{h}")
                    for a in range(tiles_):
                        g = tiles_ * h + a
                        ins_ = stt(o[:, g, :], o[:, g, :], par[:, g0 + g:g0 + g + 1], bk[:, 0:T], ALU.mult, ALU.mult)
                    free_step(ins_, f"{l}nb{h}")
                    for a in range(tiles_):
                        g = tiles_ * h + a
                        ve.wait_ge(*copied(f"{l}r{g}"))
                        ve.tensor_tensor(o[:, g, :], o[:, g, :], gate_r[:, g, :], ALU.mult).then_inc(gated_ready, 1)

            ve.wait_ge(const_ready, N_CONST)
            for kt in range(KT):
                free(ve.tensor_copy(xT[:, kt, :], take(f"x{kt}")[:, 0:T]), f"x{kt}")
            free_step(ve.tensor_copy(par[:, :], take("par")[:, 0:52]), "par")
            ve.wait_ge(small_loaded, N_SMALL)

            norm(0, "L0ss")
            for h in range(4):
                free_step(ve.tensor_scalar(t1[:, h, :], take(f"L0z{h}")[:, 0:T], par[:, 32 + h:33 + h], None, ALU.add), f"L0z{h}")
                stt(t2[:, h, :], t1[:, h, :], -1.0, t1[:, h, :], ALU.mult, ALU.max).then_inc(abs_ready, 1)
            for h in range(4):
                ve.wait_ge(ln_ready, h + 1)
                step(stt(t1[:, h, :], t1[:, h, :], 0.0, t2[:, h, :], ALU.min, ALU.subtract))
                ve.tensor_tensor_scan(cum[:, h, :], going[:, :], t1[:, h, :], 0.0, ALU.mult, ALU.add).then_inc(cum_ready, 1)
            ve.wait_ge(cum_ready, 4)

            def chunks(t):
                a, n, _ = t.shape
                return ((t[:, :, 0:NP_].rearrange("p h (c t) -> p h c t", c=NC),
                         t[:, :, L - 1:NP_:L].unsqueeze(3).broadcast_to([a, n, NC, L])),
                        (t[:, :, NP_:T].rearrange("p h (c t) -> p h c t", c=NB),
                         t[:, :, NP_ + NS - 1:T:NS].unsqueeze(3).broadcast_to([a, n, NB, NS])))

            for (out, _), (x, last) in zip(chunks(t2), chunks(cum)):
                ve.tensor_tensor(out, last, x, ALU.subtract).then_inc(cum_ready, 1)
            for m in range(4):
                ve.wait_ge(*copied(f"L0q{m}"))
            ve.wait_ge(dec_ready, 1)
            ve.tensor_tensor(q0[:, :, :], q0[:, :, :], t1[:, :, :], ALU.mult).then_inc(qg_ready, 1)
            for m in range(4):
                ve.wait_ge(*copied(f"L0k{m}"))
            ve.wait_ge(dec_ready, 2)
            ve.tensor_tensor(kend[:, :, :], k0[:, :, :], t2[:, :, :], ALU.mult).then_inc(kend_ready, 1)
            ve.wait_ge(dec_ready, 5)
            ve.tensor_tensor(k0[:, :, :], k0[:, :, :], t1[:, :, :], ALU.mult).then_inc(qg_ready, 1)
            ve.wait_ge(kz_zero, 1)
            for tt in range(2):
                bk = take(f"L0kt{tt}")
                ve.tensor_copy(kz[0:64, 2 * tt, :], bk[0:64, :])
                free(ve.tensor_copy(kz[64:128, 2 * tt + 1, :], bk[64:128, :]), f"L0kt{tt}")
            free_step(ve.tensor_copy(kz[0:NSM, NC, :], take("L0kt2")[0:NSM, :]), "L0kt2")
            for tt in range(TT):
                n = TS[tt][1]
                out, m = (P0[:, tt], causal) if tt < 2 else (P0s, causal_s)
                free(ve.tensor_tensor(out, take(f"L0sc{tt}")[0:n, 0:GH * n].rearrange("p (h t) -> p h t", h=GH),
                                      over_heads(m[:, :], GH), ALU.mult), f"L0sc{tt}")
            sample_keys("L0", 0, 0)
            sample_keys("L0", 1, 0)
            for c in range(NC):
                for half, x in enumerate("ab"):
                    name = f"L0up{c}{x}"
                    bk = take(name)
                    if c == 0:
                        free_step(ve.tensor_copy(S0[:, 1, 2 * half:2 * half + 2, :], bk[:, :].rearrange("p (h v) -> p h v", h=2)), name)
                        continue
                    for a in range(2):
                        h = 2 * half + a
                        ins_ = stt(S0[:, (c + 1) % 2, h, :], S0[:, c % 2, h, :], eb[:, h, c:c + 1], bk[:, a * 256:(a + 1) * 256],
                                   ALU.mult, ALU.add)
                    free_step(ins_, name)
            for b in range(NB):
                ve.wait_ge(S_loaded[b % 3], 16 * (b // 3 + 1))
                for half, x in enumerate("ab"):
                    name = f"L0us{b}{x}"
                    bk = take(name)
                    for a in range(2):
                        h = 2 * half + a
                        ins_ = stt(Ss[:, b % 3, h, :], Ss[:, b % 3, h, :], eb[:, h, NC + b:NC + b + 1], bk[:, a * 256:(a + 1) * 256],
                                   ALU.mult, ALU.add)
                    free(ins_, name)
                if b + 2 < NB:
                    sample_keys("L0", b + 2, 0)
            ve.tensor_scalar(rows[:, 0, :], take("L0ns")[0:MH, 0:T], 1.0 / GDV, EPS, ALU.mult, ALU.add).then_inc(mean_ready, 1)
            ve.wait_ge(mean_ready, 1)
            ve.wait_ge(rowx_ready, 1)
            step(stt(rows[:, 2, :], rows[:, 0, :], -0.5, rows[:, 1, :], ALU.mult, ALU.mult))
            step(ve.tensor_tensor(rows[:, 2, :], rows[:, 2, :], rows[:, 1, :], ALU.mult))
            stt(rows[:, 0, :], rows[:, 2, :], 1.5, rows[:, 1, :], ALU.add, ALU.mult).then_inc(f_ready, 1)
            ve.tensor_copy(m_chunk[:, 2, 0:1], rows[:, 2, 0:1]).then_inc(bank_free[uses["L0ns"][0]], 1)
            gated("L0", o0, GH, 2, 36)
            residual("L0w")

            norm(1, "Fss")
            for f in range(FFT):
                ve.wait_ge(*copied(f"Fg{f}"))
                free(ve.tensor_tensor(ffa[:, f, :], ffg[:, f % 2, :], take(f"Fu{f}")[:, 0:T], ALU.mult), f"Fu{f}")
            residual("Fw")

            norm(2, "L1ss")
            free(ve.tensor_scalar(rows[:, 0, :], take("L1gi")[0:MH, 0:T], b_i[:, 0:1], None, ALU.add), "L1gi")
            free(ve.tensor_scalar(rows[:, 1, :], take("L1gf")[0:MH, 0:T], b_f[:, 0:1], None, ALU.add), "L1gf")
            ve.wait_ge(tanh_ready, 2)
            step(ve.tensor_scalar(rows[:, 0:2, :], rows[:, 0:2, :], CAPG, None, ALU.mult))
            stt(rows[:, 2, :], rows[:, 1, :], -1.0, rows[:, 1, :], ALU.mult, ALU.max).then_inc(fabs_ready, 1)
            ve.wait_ge(fln_ready, 1)
            step(stt(rows[:, 1, :], rows[:, 1, :], 0.0, rows[:, 2, :], ALU.min, ALU.subtract))
            step(ve.tensor_tensor_scan(rows[:, 3, :], going[0:MH, :], rows[:, 1, :], 0.0, ALU.mult, ALU.add))
            step(ve.tensor_tensor(rows[:, 2, :], rows[:, 0, :], rows[:, 3, :], ALU.subtract))
            step(ve.tensor_tensor_scan(rows[:, 8, :], drop[:, :], rows[:, 2, :], 0.0, ALU.add, ALU.max))

            def last_of(r, prompt):
                return rows[:, r, L - 1:NP_:L] if prompt else rows[:, r, NP_ + NS - 1:T:NS]

            step(ve.memset(m_chunk[:, 0, 0:1], 0.0))
            step(ve.tensor_tensor_scan(m_chunk[:, 1, 0:NC], last_of(8, True), last_of(3, True), 0.0, ALU.max, ALU.add))
            step(ve.tensor_copy(m_chunk[:, 0, 1:NC], m_chunk[:, 1, 0:NC - 1]))
            step(ve.tensor_tensor(m_chunk[:, 1, NC:NC + NB], last_of(8, False), m_chunk[:, 0, NC:NC + NB], ALU.max))
            step(ve.tensor_tensor(m_chunk[:, 1, NC:NC + NB], m_chunk[:, 1, NC:NC + NB], last_of(3, False), ALU.add))

            def both(out, x, y, op):
                for t0, t1_, c0, n in ((0, NP_, 0, NC), (NP_, T, NC, NB)):
                    w = (t1_ - t0) // n
                    ins_ = ve.tensor_tensor(rows[:, out, t0:t1_].rearrange("p (c t) -> p c t", c=n),
                                            rows[:, x, t0:t1_].rearrange("p (c t) -> p c t", c=n),
                                            y(c0, n).unsqueeze(2).broadcast_to([MH, n, w]), op)
                return ins_

            def m_before(c0, n):
                return m_chunk[:, 0, c0:c0 + n]

            step(both(9, 8, m_before, ALU.max))
            step(ve.tensor_scalar(rows[:, 4, :], rows[:, 9, :], -1.0, None, ALU.mult))
            both(5, 4, m_before, ALU.add)
            ve.tensor_tensor(rows[:, 6, :], rows[:, 4, :], rows[:, 3, :], ALU.subtract)
            both(7, 2, lambda c0, n: last_of(4, c0 == 0), ALU.add).then_inc(mexpo_ready, 1)

            bk = take("L1at")
            ve.tensor_copy(a_tok[:, 0:2], bk[:, 0:4 * MH].rearrange("p (t a h) -> p t a h", t=2, a=2))
            free_step(ve.tensor_copy(a_tok[0:NSM, 2], bk[0:NSM, 4 * MH:6 * MH].rearrange("p (a h) -> p a h", a=2)), "L1at")
            for j in range(4):
                ve.wait_ge(*copied(f"L1q{j}"))
                bk = take(f"L1wb{j}")
                for a in range(2):
                    r = slice(64 * a, 64 * a + 64)
                    ve.tensor_tensor(qwz[r, 2 * j + a, :], qz[r, 2 * j + a, :], bk[r, 0:T], ALU.mult).then_inc(qw_ready, 1)
                ve.tensor_copy(eb[:, j, 0:NC], bk[:, L - 1:NP_:L])
                free_step(ve.tensor_copy(eb[:, j, NC:NC + NB], bk[:, NP_ + NS - 1:T:NS]), f"L1wb{j}")
            for tt in range(TT):
                bk = take(f"L1kt{tt}")

                def weighted(c, lo, hi):
                    w = a_tok[lo:hi, tt, 1, :].unsqueeze(2).broadcast_to([hi - lo, MH, 64])
                    return ve.tensor_tensor(kz[lo:hi, c, :].rearrange("p (h k) -> p h k", h=MH),
                                            bk[lo:hi, :].rearrange("p (h k) -> p h k", h=MH), w, ALU.mult)

                if tt < 2:
                    weighted(2 * tt, 0, 64)
                    free_step(weighted(2 * tt + 1, 64, 128), f"L1kt{tt}")
                else:
                    free_step(weighted(NC, 0, NSM), "L1kt2")

            def weights_of(tt):
                n = TS[tt][1]
                halves = 2 if tt < 2 else 1
                per = MH // halves
                part = (lambda hf: f"{tt}{hf}") if tt < 2 else (lambda hf: "2")
                for hf in range(halves):
                    name = "L1db" + part(hf)
                    a = a_tok[0:n, tt, 0, per * hf:per * (hf + 1)].unsqueeze(2).broadcast_to([n, per, n])
                    free_step(ve.tensor_tensor(dmp[0:n, per * hf:per * (hf + 1), 0:n],
                                               take(name)[0:n, 0:per * n].rearrange("p (h t) -> p h t", h=per), a, ALU.add), name)
                v = dmp[0:n, :, 0:n]
                ve.tensor_scalar(v, v, 0.0, None, ALU.min).then_inc(dmp_ready, 1)
                ve.wait_ge(dexp_ready, tt + 1)
                out, m = (P1[:, tt], causal) if tt < 2 else (P1s, causal_s)
                step(ve.tensor_tensor(out, v, over_heads(m[:, :], MH), ALU.mult))
                for hf in range(halves):
                    name = "L1sc" + part(hf)
                    o = out[:, per * hf:per * (hf + 1), :]
                    free(ve.tensor_tensor(o, o, take(name)[0:n, 0:per * n].rearrange("p (h t) -> p h t", h=per), ALU.mult), name)

            weights_of(0)
            free_step(ve.tensor_copy(n_inc[:, :, :], take("L1nu")[:, 0:48].rearrange("p (j c) -> p j c", j=4)), "L1nu")
            weights_of(1)
            weights_of(2)
            ns_b = n_sm[:, :, :].unsqueeze(3).broadcast_to([P, 4, NB, NS])
            for a in range(2):
                step(ve.tensor_tensor(qn[:, a::2, :].rearrange("p j (b i) -> p j b i", b=NB),
                                      qwz[:, a::2, NP_:T].rearrange("p j (b i) -> p j b i", b=NB), ns_b, ALU.mult))
            step(ve.tensor_tensor(n_new[:, :, :], n_sm[:, :, :], eb[:, :, NC:NC + NB], ALU.mult))
            ve.tensor_tensor(n_new[:, :, :], n_new[:, :, :], n_inc[:, :, NC:NC + NB], ALU.add).then_inc(n_new_ready, 1)
            sample_keys("L1", 0, NB)
            sample_keys("L1", 1, NB)

            def add_memory(C, bk, half):
                v = bk[:, :].rearrange("p (j a v) -> p j a v", j=2, a=2)
                for a in range(2):
                    r = slice(64 * a, 64 * a + 64)
                    o = C[r, 2 * half:2 * half + 2, :]
                    ins_ = ve.tensor_tensor(o, o, v[r, :, a, :], ALU.add)
                return ins_

            for c in range(NC):
                new, old = C1[:, (c + 1) % 2], C1[:, c % 2]
                ve.wait_ge(*full(f"L1up{c}a"))
                if c == 0:
                    step(ve.memset(new, 0.0))
                    step(ve.tensor_copy(n_st[:, 1, :], n_inc[:, :, 0]))
                else:
                    step(ve.tensor_tensor(new, old, eb[:, :, c].unsqueeze(2).broadcast_to([P, 4, MDV]), ALU.mult))
                    step(ve.tensor_tensor(n_st[:, (c + 1) % 2, :], n_st[:, c % 2, :], eb[:, :, c], ALU.mult))
                    step(ve.tensor_tensor(n_st[:, (c + 1) % 2, :], n_st[:, (c + 1) % 2, :], n_inc[:, :, c], ALU.add))
                for half, x in enumerate("ab"):
                    free_step(add_memory(new, take(f"L1up{c}{x}"), half), f"L1up{c}{x}")
                ve.tensor_tensor(n_cols[:, (c + 1) % 2].rearrange("p (j a) m -> p j a m", a=2),
                                 head_col[:, :, :].rearrange("p (j a) m -> p j a m", a=2),
                                 n_st[:, (c + 1) % 2, :].unsqueeze(2).unsqueeze(3).broadcast_to([P, 4, 2, MH]), ALU.mult)\
                    .then_inc(norm_ready, 1)
            ve.tensor_copy(m_chunk[:, 2, 0:1], m_chunk[:, 1, 0:1]).then_inc(norm_ready, 1)
            for b in range(NB):
                C = Cs[:, b % 3]
                ve.wait_ge(S_loaded[b % 3], 16 * (S_LOADS[b % 3] + 2 * (b // 3) + 2))
                ve.wait_ge(*full(f"L1us{b}a"))
                step(ve.tensor_tensor(C, C, eb[:, :, NC + b].unsqueeze(2).broadcast_to([P, 4, MDV]), ALU.mult))
                for half, x in enumerate("ab"):
                    free(add_memory(C, take(f"L1us{b}{x}"), half), f"L1us{b}{x}")
                if b + 2 < NB:
                    sample_keys("L1", b + 2, NB)
            free_step(ve.tensor_copy(rows[:, 8, :], take("L1den")[0:MH, 0:T]), "L1den")
            step(stt(rows[:, 9, :], rows[:, 8, :], -1.0, rows[:, 8, :], ALU.mult, ALU.max))
            step(ve.tensor_tensor(rows[:, 9, :], rows[:, 9, :], rows[:, 6, :], ALU.max))
            step(ve.reciprocal(rows[:, 9, :], rows[:, 9, :]))
            free_step(ve.tensor_tensor(rows[:, 0, :], take("L1ns")[0:MH, 0:T], rows[:, 9, :], ALU.mult), "L1ns")
            step(ve.tensor_tensor(rows[:, 0, :], rows[:, 0, :], rows[:, 9, :], ALU.mult))
            ve.tensor_scalar(rows[:, 0, :], rows[:, 0, :], 1.0 / MDV, EPS, ALU.mult, ALU.add).then_inc(mean_ready, 1)
            ve.wait_ge(mean_ready, 2)
            ve.wait_ge(rowx_ready, 2)
            polish(rows[:, 0, :], rows[:, 1, :], rows[:, 2, :], step)
            ve.tensor_tensor(rows[:, 0, :], rows[:, 1, :], rows[:, 9, :], ALU.mult).then_inc(f_ready, 1)
            gated("L1", num, MH, 1, 44)
            residual("L1w")

            for i in range(3):
                ve.wait_ge(S_stored[i], 16 * 3 * S_LOADS[i])
            ve.wait_ge(prompt_C_stored, 32)
            ve.memset(h_tok[:, 2, :], 0.0).then_inc(tok_cleared, 1)
            ve.memset(x_acc[:, 2, :], 0.0)
            ve.memset(ye[:, :], 0.0)
            ve.memset(selT[:, :], 0.0).then_inc(pad_zero, 1)
            step(ve.memset(lg[:, :, :], 0.0))
            step(ve.memset(chosen[:, :, :], 0.0))
            norm(3, "Mss")
            bk = take("Mlog")
            ve.tensor_tensor(lg[:, 0:2, :], bk[:, 0:2 * NE].rearrange("p (t e) -> p t e", t=2),
                             b_rt[:, :].unsqueeze(1).broadcast_to([P, 2, NE]), ALU.add)
            free_step(ve.tensor_tensor(lg[0:NSM, 2, :], bk[0:NSM, 2 * NE:3 * NE], b_rt[0:NSM, :], ALU.add), "Mlog")

            def spread(col):
                c = col if len(col.shape) == 3 else col.unsqueeze(2)
                return c.broadcast_to([P, TT, NE])

            step(ve.tensor_reduce(st[:, 0, :], lg[:, :, :], AX_X, ALU.max))
            ve.tensor_tensor(lg[:, :, :], lg[:, :, :], spread(st[:, 0, :]), ALU.subtract).then_inc(logit_ready, 1)
            ve.wait_ge(prob_ready, 1)
            step(ve.tensor_reduce(st[:, 1, :], pr[:, :, :], AX_X, ALU.add))
            step(ve.reciprocal(st[:, 1, :], st[:, 1, :]))
            step(ve.tensor_tensor(pr[:, :, :], pr[:, :, :], spread(st[:, 1, :]), ALU.mult))
            for tt in range(TT):
                step(ve.max(top_p[:, tt, :], pr[:, tt, :]))
                step(ve.max_index(top_i[:, tt, :], top_p[:, tt, :], pr[:, tt, :]))
            step(ve.tensor_copy(top_f[:, :, :], top_i[:, :, :]))
            e_no = expert_no[:, :].unsqueeze(1).broadcast_to([P, TT, NE])
            step(ve.tensor_tensor(oh1[:, :, :], e_no, spread(top_f[:, :, 0:1]), ALU.is_equal))
            step(ve.tensor_tensor(oh2[:, :, :], e_no, spread(top_f[:, :, 1:2]), ALU.is_equal))
            ve.tensor_tensor(chosen[:, 0:2, :], oh1[:, 0:2, :], oh2[:, 0:2, :], ALU.add)
            ve.tensor_tensor(chosen[0:NSM, 2, :], oh1[0:NSM, 2, :], oh2[0:NSM, 2, :], ALU.add).then_inc(chosen_ready, 1)
            step(ve.tensor_tensor(st[:, 2, :], top_p[:, :, 0], top_p[:, :, 1], ALU.add))
            step(ve.reciprocal(st[:, 3, :], st[:, 2, :]))
            step(ve.tensor_tensor(oh1[:, :, :], oh1[:, :, :], spread(top_p[:, :, 0:1]), ALU.mult))
            step(ve.tensor_tensor(oh2[:, :, :], oh2[:, :, :], spread(top_p[:, :, 1:2]), ALU.mult))
            step(ve.tensor_tensor(gates[:, :, :], oh1[:, :, :], oh2[:, :, :], ALU.add))
            step(ve.tensor_tensor(gates[:, :, :], gates[:, :, :], spread(st[:, 3, :]), ALU.mult))
            for kt in range(KT):
                bk = take(f"Mx{kt}")
                ve.tensor_copy(x_acc[:, 0:2, kt * P:(kt + 1) * P], bk[:, 0:2 * P].rearrange("p (a b) -> p a b", a=2))
                free(ve.tensor_copy(x_acc[0:NSM, 2, kt * P:(kt + 1) * P], bk[0:NSM, 2 * P:3 * P]), f"Mx{kt}")
            bk = take("Mrank")
            stt(place[:, :, :], bk[:, 0:TT * NE].rearrange("p (t e) -> p t e", t=TT), BIG, chosen[:, :, :], ALU.add, ALU.mult)
            free_step(ve.tensor_copy(count[:, :], bk[:, TT * NE:(TT + 1) * NE]), "Mrank")
            step(ve.tensor_scalar(place[:, :, :], place[:, :, :], -BIG, None, ALU.add))
            pos3 = tab_pos[:, :].rearrange("p (i t) -> p t i", t=TT)
            gate3 = tab_gate[:, :].rearrange("p (i t) -> p t i", t=TT)
            step(ve.tensor_copy(pos3[:, :, 0:NE], place[:, :, :]))
            step(ve.tensor_copy(gate3[:, :, 0:NE], gates[:, :, :]))

            def select(at, ready):
                for tt in range(TT):
                    ins_ = ve.tensor_scalar(sel[:, tt, :], slot_no[:, :], tab_pos[:, at(tt)], None, ALU.is_equal)
                ins_.then_inc(ready, 1)

            select(lambda tt: slice(tt, tt + 1), sel_ready)
            step(ve.tensor_tensor(flag[:, :, :], count[:, :].unsqueeze(1).broadcast_to([P, 2, NE]), cand_skip[:, :, :], ALU.is_gt))
            f16 = flag[:, :, :].rearrange("p k e -> p (k e)")
            o16 = order[:, :, :].rearrange("p k e -> p (k e)")
            e16 = cand_e[:, :, :].rearrange("p k e -> p (k e)")
            step(ve.tensor_tensor_scan(o16, ones[:, 0:2 * NE], f16, 0.0, ALU.mult, ALU.add))
            step(ve.tensor_scalar(tab_f[:, 15:16], o16[:, 2 * NE - 1:2 * NE], float(NE), None, ALU.add))
            step(ve.tensor_tensor(o16, o16, f16, ALU.mult))
            step(ve.tensor_tensor(pick[:, :, :], o16.unsqueeze(1).broadcast_to([P, MORE, 2 * NE]),
                                  more_no[:, :].unsqueeze(2).broadcast_to([P, MORE, 2 * NE]), ALU.is_equal))

            def picked_value(out, v16):
                step(ve.tensor_tensor(picked[:, :, :], pick[:, :, :], v16.unsqueeze(1).broadcast_to([P, MORE, 2 * NE]), ALU.mult))
                step(ve.tensor_reduce(out, picked[:, :, :], AX_X, ALU.add))

            step(ve.tensor_copy(tab_f[:, 0:NE], expert_no[:, :]))
            step(ve.memset(tab_f[:, NE + MORE:15], 0.0))
            picked_value(tab_f[:, NE:NE + MORE], e16)
            for tt in range(TT):
                step(ve.tensor_tensor(cand_v[:, :, :], place[:, tt, :].unsqueeze(1).broadcast_to([P, 2, NE]), cand_skip[:, :, :], ALU.subtract))
                picked_value(pos3[:, tt, NE:NE + MORE], cand_v[:, :, :].rearrange("p k e -> p (k e)"))
                step(ve.tensor_copy(cand_v[:, :, :], gates[:, tt, :].unsqueeze(1).broadcast_to([P, 2, NE])))
                picked_value(gate3[:, tt, NE:NE + MORE], cand_v[:, :, :].rearrange("p k e -> p (k e)"))
            ve.tensor_copy(tab_i[:, :], tab_f[:, :]).then_inc(table_ready, 1)

            def tokens_in(half, bk):
                return ve.tensor_copy(xg[:, 4 * half:4 * half + 4, :], bk[:, 0:4 * CAP].rearrange("p (k c) -> p k c", k=4))

            for half in range(2):
                free(tokens_in(half, take(f"Mga{half}")), f"Mga{half}")
            ve.wait_ge(table_ready, 1)
            n_items = ve.value_load(tab_i[0:1, 15:16], min_val=NE, max_val=NE + MORE)

            def add_pass(i):
                for n in range(6):
                    tt, half = n // 2, n % 2
                    b, m = SCB[n % 2], TS[tt][1]
                    ve.wait_ge(*loop_full(b, n // 2, i))
                    o = x_acc[0:m, tt, half * 512:(half + 1) * 512]
                    ve.tensor_tensor(o, o, psum[b][0:m, :], ALU.add).then_inc(bank_free[b], 1)

            with ve.Fori(0, n_items) as i:
                for s in range(STEPS):
                    b = GU[s % 2]
                    ve.wait_ge(silu_ready, i * STEPS + (s + 1))
                    ve.tensor_tensor(act[:, s % 2, :, :].rearrange("p f c -> p (f c)"), sg[:, s % 2, :],
                                     psum[b][:, 2 * CAP:4 * CAP], ALU.mult).then_inc(bank_free[b], 1)
                    if s == 0:
                        add_pass(i)
                    if s == 4:
                        for tt in range(TT):
                            ins_ = ve.tensor_scalar(selg[:, tt, :], slot_no[:, :], tab_pos[:, bass.ds(i * TT + tt, 1)],
                                                    tab_gate[:, bass.ds(i * TT + tt, 1)], ALU.is_equal, ALU.mult)
                        ins_.then_inc(selg_ready, 1)
                        select(lambda tt: bass.ds(i * TT + (TT + tt), 1), sel_ready)
                ve.wait_ge(*loop_full(TPB, 0, i))
                ve.tensor_copy(selT[:, :], psum[TPB][0:CAP, 0:TT * P]).then_inc(bank_free[TPB], 1)
                for half in range(2):
                    ve.wait_ge(*loop_full(GAB[half], half, i))
                    tokens_in(half, psum[GAB[half]]).then_inc(bank_free[GAB[half]], 1)
            add_pass(n_items)

            ve.wait_ge(fsq_ready, 3)
            ve.tensor_scalar(st[:, 4, :], st[:, 4, :], 1.0 / D, EPS, ALU.mult, ALU.add).then_inc(fmean_ready, 1)
            ve.wait_ge(fmean_ready, 1)
            ve.wait_ge(finv_ready, 1)
            polish(st[:, 4, :], st[:, 5, :], st[:, 3, :], step)
            for tt, (t0, n) in enumerate(TS):
                stt(x_acc[0:n, tt, :], x_acc[0:n, tt, :], st[0:n, 5, tt:tt + 1], g_final[0:n, :], ALU.mult, ALU.mult)\
                    .then_inc(out_ready, 1)


_INS = ["x_prompt", "x_sample", "state_gla_S", "state_mlstm_C", "state_mlstm_n", "state_mlstm_m",
        "norm_mix", "norm_ffn", "norm_final", "gla_w_in", "gla_w_a2", "gla_b_a", "gla_g_norm", "gla_w_out",
        "mlstm_w_in", "mlstm_b_gate", "mlstm_g_norm", "mlstm_w_out", "ffn_w_gu", "ffn_w_down",
        "moe_w_router", "moe_b_router", "moe_w_gu", "moe_w_down"]
_OUTS = [(1, NP_, D), (NB, NS, D), (1, 1, GH, P, GDV), (1, 1, MH, 64, MDV), (1, 1, MH, 64), (1, 1, MH),
         (1, NB, GH, P, GDV), (1, NB, MH, 64, MDV), (1, NB, MH, 64), (1, NB, MH)]


def kernel(**inputs):
    import numpy as _np
    import concourse.bacc as _bacc
    from concourse import mybir as _mybir
    from concourse.bass_utils import run_bass_kernel_spmd as _run

    nc = _bacc.Bacc("TRN2", target_bir_lowering=False, num_devices=1)
    arrays, ins, outs = {}, {}, []
    for name in _INS:
        a = _np.ascontiguousarray(inputs[name])
        arrays[f"in_{name}_dram"] = a
        ins[name] = nc.dram_tensor(f"in_{name}_dram", a.shape, _mybir.dt.from_np(a.dtype), kind="ExternalInput").ap()
    for i, shape in enumerate(_OUTS):
        outs.append(nc.dram_tensor(f"out_{i}_dram", shape, _mybir.dt.float32, kind="ExternalOutput").ap())
    trunk_kernel(nc, ins, outs)
    r = _run(nc, [arrays], core_ids=[0])
    return tuple(r.results[0][f"out_{i}_dram"] for i in range(len(_OUTS)))
```

```python
from contextlib import ExitStack

import concourse.bass as bass
from concourse import mybir

F32 = mybir.dt.float32
F32R = mybir.dt.float32r
I32 = mybir.dt.int32
U32 = mybir.dt.uint32
ALU = mybir.AluOpType
ACT = mybir.ActivationFunctionType
AX_X = mybir.AxisListType.X

P = 128
D = 1024
KT = D // P
NP_, NB, NS = 256, 8, 4
NSM = NB * NS
T = NP_ + NSM
L = 64
NC = NP_ // L
TT = 3
TS = [(0, P), (P, P), (NP_, NSM)]
QK = 512
GH, GDV = 4, 256
MH, MDV = 8, 128
RANK = 16
TAU = 16.0
CAPG = 15.0
FF = 2816
NE, FE = 8, 3584
EPS = 1e-6
CAP = 96
MORE = 5
ITEMS = NE + MORE + 1
SLOT = 2048
COLS = SLOT // KT
RING = 7
SPLIT = 3
HI_SLOTS = 3
N_QKV = 2 * QK // COLS + D // COLS
FFT = FF // P
FBLK = FF // COLS
DG = [(0, 8), (8, 8), (16, 6)]
N_MIX = 2 * QK // COLS + 2 * D // COLS + D // COLS
N_FFN = 2 * FBLK + (D // COLS) * len(DG)
N_STATIC = 2 * N_MIX + N_FFN
WIDE = 512
STEPS = FE // WIDE
HALF = KT // 2
PER = 6 * STEPS
WORK = 24576
BIG = 1024.0


def bank_plan():
    uses, turns = {}, [0] * 8

    def use(name, bank):
        uses[name] = (bank, turns[bank])
        turns[bank] += 1

    use("par", 7)
    for kt in range(KT):
        use(f"x{kt}", kt % 7)
    for layer in range(2):
        l = f"L{layer}"
        use(l + "ss", 3)
        n = 0

        def pj(name):
            nonlocal n
            use(l + name, n % 3)
            n += 1

        if layer == 0:
            pj("lr")
        else:
            pj("gi")
            pj("gf")
        for m in range(4):
            pj(f"q{m}")
        if layer == 0:
            for m in range(4):
                use(f"L0z{m}", 4 + m)
        for m in range(4):
            pj(f"k{m}")
        for s in range(D // COLS):
            for tt in range(TT):
                pj(f"v{s}{tt}")
        if layer == 1:
            use("L1at", 3)
            for j in range(4):
                use(f"L1wb{j}", 4 + j)
        for tt in range(TT):
            use(l + f"kt{tt}", 4 + tt)
        if layer == 0:
            for tt in range(TT):
                use(l + f"sc{tt}", 3)
        else:
            use("L1nu", 7)
            for tt in range(2):
                for hf in range(2):
                    use(f"L1db{tt}{hf}", 3 + hf)
                for hf in range(2):
                    use(f"L1sc{tt}{hf}", 5 + hf)
            use("L1db2", 3)
            use("L1sc2", 5)
        for m in range(8):
            pj(f"r{m}")
        for c in range(NC):
            use(l + f"up{c}a", 6)
            use(l + f"up{c}b", 7)
        for tt in range(2):
            use(l + f"o{tt}a", 4)
            use(l + f"o{tt}b", 5)
        use(l + "o2", 4)
        if layer == 1:
            use("L1den", 3)
        for b in range(NB):
            use(l + f"us{b}a", 6)
            use(l + f"us{b}b", 7)
        use(l + "ns", 5)
        for h in range(GH if layer == 0 else MH):
            use(l + f"nb{h}", h % 3)
        for m in range(8):
            use(l + f"w{m}", 3 + m % 5)
        if layer == 0:
            use("Fss", 3)
            for f in range(FFT):
                base = 0 if (f % 2 == 0) else 4
                use(f"Fg{f}", base)
                use(f"Fu{f}", base + 1)
            for m in range(8):
                use(f"Fw{m}", [2, 3, 6, 7][m % 4])
    use("Mss", 3)
    use("Mlog", 0)
    for kt in range(KT):
        use(f"Mh{kt}", kt)
    for kt in range(KT):
        use(f"Mx{kt}", kt)
    use("Mrank", 0)
    use("Mga0", 1)
    use("Mga1", 3)
    return uses, turns


GB, UB, YB, TB, MB = (0, 1), (2, 3), (4, 5), 6, 7
GAB = (GB[1], UB[1])
LOOP_TURNS = {0: 4, 1: 4, 2: 4, 3: 4, 4: 1, 5: 1, 6: STEPS, 7: 7}


def trunk_kernel(nc, ins, outs):
    uses, static_turns = bank_plan()
    (y_p, y_s, S_p, C_p, n_p, m_p, S_s, C_s, n_s, m_s) = outs

    with ExitStack() as ctx:
        def sb(name, shape, dt=F32):
            return ctx.enter_context(nc.sbuf_tensor(name, shape, dt))

        def sem(name):
            return ctx.enter_context(nc.semaphore(name))

        with nc.sbuf_tensor("ring", [P, RING * SLOT], F32) as ring:
            pass
        ring_lo = sb("ring_lo", [P, RING * SLOT], F32R)
        xT = sb("xT", [P, KT, T])
        hT = sb("hT", [P, KT, T])
        rbc = sb("rbc", [P, 2, T])
        psum = [ctx.enter_context(nc.psum_tensor(f"bank{b}", [P, 512], F32)) for b in range(8)]

        ident = sb("ident", [P, P])
        ones = sb("ones", [P, P])
        before = sb("before", [P, P])
        causal = sb("causal", [P, P])
        causal_s = sb("causal_s", [NSM, NSM])
        batch_of = sb("batch_of", [NSM, NB])
        going = sb("going", [P, T])
        drop = sb("drop", [MH, T])
        head_row = sb("head_row", [MH, MH, P])
        pair_row = sb("pair_row", [MH, 4, P])
        head_col = sb("head_col", [P, MH, MH])
        slot_no = sb("slot_no", [P, CAP])
        expert_no = sb("expert_no", [P, NE])
        cand_e = sb("cand_e", [P, 2, NE])
        cand_skip = sb("cand_skip", [P, 2, NE])
        more_no = sb("more_no", [P, MORE])
        one_col = sb("one_col", [P, 2])

        par_rows = sb("par_rows", [52, P])
        par = sb("par", [P, 52])
        g_final = sb("g_final", [P, D])
        w_lr = sb("w_lr", [P, KT, RANK])
        w_gate = sb("w_gate", [P, KT, 2 * MH])
        w_a2 = sb("w_a2", [RANK, QK])
        w_rt = sb("w_rt", [P, KT, NE])
        b_rt = sb("b_rt", [P, NE])
        b_i = sb("b_i", [MH, 1])
        b_f = sb("b_f", [MH, 1])
        lr_sb = sb("lr_sb", [RANK, T])
        eb = sb("eb", [P, 4, NC + NB])

        rows = sb("rows", [MH, 10, T])
        m_chunk = sb("m_chunk", [MH, 3, NC + NB])
        a_tok = sb("a_tok", [P, TT, 2, MH])
        n_st = sb("n_st", [P, 2, 4])
        n_sm = sb("n_sm", [P, 4, NB])
        n_new = sb("n_new", [P, 4, NB])
        n_inc = sb("n_inc", [P, 4, NC + NB])
        n_cols = sb("n_cols", [P, 2, MH, MH])

        lg = sb("lg", [P, TT, NE])
        pr = sb("pr", [P, TT, NE])
        top_p = sb("top_p", [P, TT, NE])
        top_i = sb("top_i", [P, TT, NE], U32)
        top_f = sb("top_f", [P, TT, NE])
        st = sb("st", [P, 6, TT])
        oh1 = sb("oh1", [P, TT, NE])
        oh2 = sb("oh2", [P, TT, NE])
        gates = sb("gates", [P, TT, NE])
        chosen = sb("chosen", [P, TT, NE])
        place = sb("place", [P, TT, NE])
        count = sb("count", [P, NE])
        flag = sb("flag", [P, 2, NE])
        order = sb("order", [P, 2, NE])
        pick = sb("pick", [P, MORE, 2 * NE])
        picked = sb("picked", [P, MORE, 2 * NE])
        cand_v = sb("cand_v", [P, 2, NE])
        tab_pos = sb("tab_pos", [P, ITEMS * TT])
        tab_gate = sb("tab_gate", [P, ITEMS * TT])
        tab_f = sb("tab_f", [P, 16])
        tab_i = sb("tab_i", [P, 16], I32)

        with nc.sbuf_tensor("work", [P, WORK], F32) as work_mem:
            work = work_mem
        with nc.sbuf_tensor("work_split", [P, WORK], F32R) as work_split_mem:
            work_split = work_split_mem

        def area(at, *dims, rows_=P, of=None):
            n = 1
            for d in dims:
                n *= d
            v = (work if of is None else of)[0:rows_, at:at + n]
            if len(dims) == 2:
                v = v.rearrange("p (a b) -> p a b", a=dims[0])
            if len(dims) == 3:
                v = v.rearrange("p (a b c) -> p a b c", a=dims[0], b=dims[1])
            return v

        xtok = area(9216, TT, D)
        q0 = area(0, 4, T)
        k0 = area(1152, 4, T)
        cum = area(2304, 4, T)
        kend = area(3456, 4, T)
        t1 = area(4608, 4, T)
        t2 = area(5760, 4, T)
        o0 = area(4608, 8, T)
        sq0 = area(2304, 8, T)
        gate_r = area(6912, 8, T)
        v_tok = area(9216, TT, D)
        kz = area(12288, NC + 1, QK)
        P0 = area(14848, 2, GH, P)
        P0s = area(14848 + 1024, GH, NSM, rows_=NSM)
        S0 = area(16000, 2, GH, GDV)
        Ss = area(18048, 3, GH, GDV)
        kb = area(21120, 2, QK, rows_=NSM)
        qz = area(0, MH, T)
        qwz = area(2304, MH, T)
        k1 = area(4608, 4, T)
        dmp = area(5760, MH, P)
        P1 = area(14848, 2, MH, P)
        P1s = area(14848 + 2048, MH, NSM, rows_=NSM)
        C1 = area(17152, 2, 4, MDV)
        Cs = area(18176, 3, 4, MDV)
        qn = area(19712, MH, NSM)
        num = area(22144, MH, T)
        sq1 = area(0, MH, T)
        mh_hi = area(12288, KT, T, of=work_split)
        mh_lo = area(14592, KT, T, of=work_split)
        mw_hi = area(16896, HI_SLOTS, SLOT, of=work_split)
        fw_hi = area(6912, HI_SLOTS, SLOT, of=work_split)
        ffa_hi = area(0, FFT, T, of=work_split)
        ffa_lo = area(13056, FFT, T, of=work_split)
        h_hi = area(19392, KT, T, of=work_split)
        h_lo = area(21696, KT, T, of=work_split)
        ffg = area(24000, 2, T)
        ffp = rbc
        expert_mem = ExitStack()
        ctx.enter_context(expert_mem)

        def es(name, shape, dt=F32):
            return expert_mem.enter_context(nc.sbuf_tensor(name, shape, dt))

        w_hi = es("w_hi", [P, SPLIT, SLOT], F32R)
        w_lo = es("w_lo", [P, SPLIT, SLOT], F32R)
        xg_hi = es("xg_hi", [P, KT, CAP], F32R)
        xg_lo = es("xg_lo", [P, KT, CAP], F32R)
        aT_hi = es("aT_hi", [P, 4, CAP], F32R)
        aT_lo = es("aT_lo", [P, 4, CAP], F32R)
        h_tok = es("h_tok", [P, TT, D])
        x_acc = es("x_acc", [P, TT, D])
        sg = es("sg", [CAP, 2, WIDE])
        act = es("act", [CAP, WIDE])
        ye = es("ye", [CAP, D])
        selT = es("selT", [CAP, TT * P])
        sel = es("sel", [P, TT, CAP])
        selg = es("selg", [P, TT, CAP])

        const_ready = sem("const_ready")
        par_loaded = sem("par_loaded")
        small_loaded = sem("small_loaded")
        x_loaded = sem("x_loaded")
        kz_zero = sem("kz_zero")
        qz_zero = sem("qz_zero")
        slot_loaded = [sem(f"slot_loaded{s}") for s in range(RING)]
        fhi_ready = sem("fhi_ready")
        flo_ready = sem("flo_ready")
        mlo_ready = sem("mlo_ready")
        hhi_ready = sem("hhi_ready")
        hlo_ready = sem("hlo_ready")
        ffa_ready = sem("ffa_ready")
        whi_ready = sem("whi_ready")
        wlo_ready = sem("wlo_ready")
        hi_ready = sem("hi_ready")
        split_used = sem("split_used")
        part_used = sem("part_used")
        bank_full = [sem(f"bank_full{b}") for b in range(8)]
        bank_free = [sem(f"bank_free{b}") for b in range(8)]
        v_chain = sem("v_chain")
        a_chain = sem("a_chain")
        sq_ready = sem("sq_ready")
        inv_ready = sem("inv_ready")
        h_ready = sem("h_ready")
        abs_ready = sem("abs_ready")
        ln_ready = sem("ln_ready")
        cum_ready = sem("cum_ready")
        dec_ready = sem("dec_ready")
        qg_ready = sem("qg_ready")
        kend_ready = sem("kend_ready")
        S_loaded = [sem(f"S_loaded{i}") for i in range(3)]
        S_stored = [sem(f"S_stored{i}") for i in range(3)]
        kb_ready = sem("kb_ready")
        osq_ready = sem("osq_ready")
        mean_ready = sem("mean_ready")
        rowx_ready = sem("rowx_ready")
        f_ready = sem("f_ready")
        gated_ready = sem("gated_ready")
        tanh_ready = sem("tanh_ready")
        fabs_ready = sem("fabs_ready")
        fln_ready = sem("fln_ready")
        mexpo_ready = sem("mexpo_ready")
        mexp_ready = sem("mexp_ready")
        q_half = sem("q_half")
        dmp_ready = sem("dmp_ready")
        dexp_ready = sem("dexp_ready")
        qw_ready = sem("qw_ready")
        norm_ready = sem("norm_ready")
        n_new_ready = sem("n_new_ready")
        prompt_S_stored = sem("prompt_S_stored")
        prompt_C_stored = sem("prompt_C_stored")
        small_stored = sem("small_stored")
        pad_zero = sem("pad_zero")
        tok_cleared = sem("tok_cleared")
        logit_ready = sem("logit_ready")
        prob_ready = sem("prob_ready")
        chosen_ready = sem("chosen_ready")
        table_ready = sem("table_ready")
        sel_ready = sem("sel_ready")
        selg_ready = sem("selg_ready")
        fsq_ready = sem("fsq_ready")
        fmean_ready = sem("fmean_ready")
        finv_ready = sem("finv_ready")
        out_ready = sem("out_ready")
        out_stored = sem("out_stored")

        N_CONST = 36
        N_FIRST = 5
        N_SMALL = 16 * 17
        S_LOADS = [3, 3, 2]

        def slot(i):
            s = i % RING
            return ring[:, s * SLOT:(s + 1) * SLOT], s

        def expert_slot(j):
            return slot(N_STATIC + j)

        def loads_before(s):
            return len(range(s, N_STATIC, RING))

        def full(name):
            b, k = uses[name]
            return bank_full[b], k + 1

        def copied(name):
            b, k = uses[name]
            return bank_free[b], k + 1

        def loop_full(b, k, i):
            return bank_full[b], i * LOOP_TURNS[b] + (static_turns[b] + k + 1)

        def loop_before(b, k, i):
            return bank_free[b], i * LOOP_TURNS[b] + (static_turns[b] + k)

        def mixer_loads(l, w_in, w_out):
            v = w_in[0].rearrange("(t p) n -> p t n", p=P)
            last = [f"{l}{w}{m}" for w in "qk" for m in (1, 3)] + [f"{l}v{s}2" for s in range(4)] \
                + [f"{l}r{m}" for m in (1, 3, 5, 7)]
            for c, name in enumerate(last):
                yield v[:, :, c * COLS:(c + 1) * COLS], full(name)
            v = w_out[0].rearrange("(t p) n -> p t n", p=P)
            for c in range(D // COLS):
                yield v[:, :, c * COLS:(c + 1) * COLS], full(f"{l}w{2 * c + 1}")

        def ffn_loads():
            v = ins["ffn_w_gu"][0].rearrange("(t p) n -> p t n", p=P)
            for c in range(FBLK):
                for o, x in ((0, "g"), (FF, "u")):
                    yield v[:, :, o + c * COLS:o + (c + 1) * COLS], full(f"F{x}{2 * c + 1}")
            v = ins["ffn_w_down"][0].rearrange("(t p) n -> p t n", p=P)
            for c in range(D // COLS):
                for g, (f, k) in enumerate(DG):
                    yield v[:, f:f + k, c * COLS:(c + 1) * COLS], \
                        (part_used, 2 * c + g + 1) if g < 2 else full(f"Fw{2 * c + 1}")

        static_loads = [*mixer_loads("L0", ins["gla_w_in"], ins["gla_w_out"]), *ffn_loads(),
                        *mixer_loads("L1", ins["mlstm_w_in"], ins["mlstm_w_out"])]
        assert len(static_loads) == N_STATIC

        PART_AT, PART_N, PART_BEFORE = (0, N_MIX, N_MIX + N_FFN), (N_QKV, N_FFN, N_QKV), (0, N_QKV, N_QKV + N_FFN)

        def split_parts(g, n):
            raw, s = slot(PART_AT[g] + n)
            w = COLS * (DG[(n - 2 * FBLK) % len(DG)][1] if g == 1 and n >= 2 * FBLK else KT)
            return raw[:, 0:w], (fw_hi if g == 1 else mw_hi)[:, n % HI_SLOTS, 0:w], ring_lo[:, s * SLOT:s * SLOT + w]

        expert_order = [(k, 0, x) for k in "gu" for x in range(2)]
        for j in range(1, STEPS):
            expert_order += [(k, j - (k == "d"), x) for k in "gud" for x in range(2)]
        expert_order += [("d", STEPS - 1, x) for x in range(2)]
        assert len(expert_order) == PER
        expert_at = {x: n for n, x in enumerate(expert_order)}

        def by_half(ap, a):
            return ap.rearrange("(j a) k v -> a k j v", a=2)[a]

        def split_free(eng, j, i):
            if j < SPLIT:
                used_ = i * SPLIT_COUNT + 1
                if j == SPLIT - 1:
                    eng.wait_ge(bank_full[YB[1]], i + static_turns[YB[1]])
                    return
            else:
                kind, nth, x = expert_order[j - SPLIT]
                if kind != "d" and x == 1:
                    eng.wait_ge(*loop_full((GB if kind == "g" else UB)[nth % 2], nth // 2, i))
                    return
                used_ = i * SPLIT_COUNT + (split_counts[j - SPLIT] + 1)
            eng.wait_ge(split_used, used_)

        split_counts, SPLIT_COUNT = {}, 0
        for j, (kind, nth, x) in enumerate(expert_order):
            if (kind != "d" and x == 0) or (kind == "d" and j < PER - 1):
                SPLIT_COUNT += 1
                split_counts[j] = SPLIT_COUNT
        HI_TURNS = STEPS + 2

        def turned_hi(ac, nth, i):
            ac.wait_ge(*loop_full(TB, nth, i))
            ac.activation(aT_hi[:, :, :], psum[TB][:, 0:4 * CAP].rearrange("p (f c) -> p f c", f=4), ACT.Copy).then_inc(hi_ready, 1)

        block = ctx.enter_context(nc.Block())

        @block.sync
        def _(sp):
            def small(dst, src, done=small_loaded):
                sp.dma_start(dst, src, allow_slow_non_contiguous=True).then_inc(done, 16)

            small(par_rows[0:16, :], ins["norm_mix"].rearrange("l (t p) -> (l t) p", p=P), par_loaded)
            small(par_rows[16:32, :], ins["norm_ffn"].rearrange("l (t p) -> (l t) p", p=P), par_loaded)
            small(par_rows[32:36, :], ins["gla_b_a"].rearrange("l (t p) -> (l t) p", p=P), par_loaded)
            small(par_rows[36:44, :], ins["gla_g_norm"].rearrange("l h (t p) -> (l h t) p", p=P), par_loaded)
            small(par_rows[44:52, :], ins["mlstm_g_norm"].rearrange("l h p -> (l h) p"), par_loaded)
            for i, (src, _) in enumerate(static_loads):
                dst, s = slot(i)
                if i == 3:
                    small(w_lr[:, :, :], ins["gla_w_in"][0, :, 3072:3088].rearrange("(t p) n -> p t n", p=P))
                    small(w_gate[:, :, :], ins["mlstm_w_in"][0, :, 3072:3088].rearrange("(t p) n -> p t n", p=P))
                    small(w_a2[:, :], ins["gla_w_a2"][0])
                    small(w_rt[:, :, :], ins["moe_w_router"][0].rearrange("(t p) n -> p t n", p=P))
                    small(b_rt[:, :], ins["moe_b_router"].broadcast_to([P, NE]))
                    small(g_final[:, :], ins["norm_final"].rearrange("(a n) -> a n", a=1).broadcast_to([P, D]))
                    small(b_i[:, :], ins["mlstm_b_gate"][0, 0:MH].rearrange("(h a) -> h a", a=1))
                    small(b_f[:, :], ins["mlstm_b_gate"][0, MH:2 * MH].rearrange("(h a) -> h a", a=1))
                    small(m_chunk[:, 0, NC:NC + NB], ins["state_mlstm_m"][0].rearrange("b h -> h b"))
                    for a in range(2):
                        for j in range(4):
                            small(n_sm[64 * a:64 * a + 64, j, :], ins["state_mlstm_n"][0].rearrange("b (j a) k -> a j k b", a=2)[a, j])
                if i >= RING:
                    sp.wait_ge(*static_loads[i - RING][1])
                k, n = src.shape[1], src.shape[2]
                sp.dma_start(dst[:, 0:k * n].rearrange("p (k n) -> p k n", k=k), src).then_inc(slot_loaded[s], 16)

            w_gu, w_dn = ins["moe_w_gu"][0], ins["moe_w_down"][0]

            def load(e, j):
                kind, nth, x = expert_order[j]
                dst, s = expert_slot(j)
                if kind == "d":
                    r = nth * WIDE + x * 2 * P
                    src = w_dn[bass.ds(e, 1), r:r + 2 * P, :].rearrange("e (t p) n -> p (e t) n", p=P)
                else:
                    c = nth * WIDE + (FE if kind == "u" else 0)
                    src = w_gu[bass.ds(e, 1), x * HALF * P:(x + 1) * HALF * P, c:c + WIDE].rearrange("e (t p) n -> p (e t) n", p=P)
                out = dst.rearrange("p (k n) -> p k n", k=src.shape[1])
                sp.dma_start(out, src).then_inc(slot_loaded[s], 16)

            for j in range(PER):
                if j < RING:
                    sp.wait_ge(*static_loads[N_STATIC + j - RING][1])
                else:
                    sp.wait_ge(wlo_ready, j - RING + 1)
                load(0, j)

            def load_pass(i, e):
                for j in range(PER):
                    sp.wait_ge(wlo_ready, i * PER + (j - RING + 1))
                    load(e, j)

            with sp.Fori(1, NE - 1) as e:
                load_pass(e, e)
            sp.wait_ge(table_ready, 1)
            n_items = sp.value_load(tab_i[0:1, 15:16], min_val=NE, max_val=NE + MORE)
            with sp.Fori(NE - 1, n_items) as i:
                e = sp.value_load(tab_i[0:1, bass.ds(i, 1)], min_val=0, max_val=NE - 1)
                load_pass(i, e)

        @block.gpsimd
        def _(gp):
            made = [0]

            def c(ins_):
                made[0] += 1
                ins_.then_inc(const_ready, 1)
                gp.wait_ge(const_ready, made[0])

            def keep(t, op, pattern, mult, base=0, fill=0.0):
                c(gp.affine_select(out=t, in_=t, compare_op=op, fill=fill, base=base, pattern=pattern,
                                   channel_multiplier=mult))

            c(gp.memset(ident[:, :], 0.0))
            keep(ident[:, :], ALU.not_equal, [[-1, P]], 1, fill=1.0)
            c(gp.memset(ones[:, :], 1.0))
            c(gp.memset(one_col[:, 0:1], 1.0))
            c(gp.memset(one_col[:, 1:2], 0.0))
            assert made[0] == N_FIRST
            c(gp.memset(before[:, :], 1.0))
            keep(before[:, :], ALU.is_gt, [[1, P]], -1)
            c(gp.memset(causal[:, :], 1.0))
            keep(causal[:, :], ALU.is_ge, [[1, P]], -1)
            keep(causal[:, :].rearrange("p (c t) -> p c t", c=2), ALU.is_ge, [[-L, 2], [0, L]], 1)
            c(gp.memset(causal_s[:, :], 1.0))
            keep(causal_s[:, :], ALU.is_ge, [[1, NSM]], -1)
            keep(causal_s[:, :].rearrange("p (c t) -> p c t", c=NB), ALU.is_ge, [[-NS, NB], [0, NS]], 1)
            c(gp.memset(batch_of[:, :], 1.0))
            keep(batch_of[:, :], ALU.is_ge, [[-NS, NB]], 1)
            keep(batch_of[:, :], ALU.is_ge, [[NS, NB]], -1, base=NS - 1)
            c(gp.memset(going[:, :], 1.0))
            c(gp.memset(going[:, 0:NP_:L], 0.0))
            c(gp.memset(going[:, NP_:T:NS], 0.0))
            c(gp.memset(drop[:, :], 0.0))
            c(gp.memset(drop[:, 0:NP_:L], -3e38))
            c(gp.memset(drop[:, NP_:T:NS], -3e38))
            c(gp.memset(head_row[:, :, :], 0.0))
            keep(head_row[:, :, :], ALU.not_equal, [[1, MH], [0, P]], -1, fill=1.0)
            c(gp.memset(pair_row[:, :, :], 0.0))
            keep(pair_row[:, :, :].rearrange("p j (a m) -> p j a m", a=2), ALU.not_equal, [[2, 4], [1, 2], [0, 64]], -1, fill=1.0)
            c(gp.memset(head_col[:, :, :], 0.0))
            keep(head_col[:, :, :], ALU.not_equal, [[1, MH], [-1, MH]], 0, fill=1.0)
            small = {"allow_small_or_imprecise_dtypes": True}
            c(gp.iota(slot_no[:, :], [[1, CAP]], 0, 0, **small))
            c(gp.iota(expert_no[:, :], [[1, NE]], 0, 0, **small))
            c(gp.iota(cand_e[:, :, :], [[0, 2], [1, NE]], 0, 0, **small))
            c(gp.iota(cand_skip[:, :, :], [[CAP, 2], [0, NE]], CAP, 0, **small))
            c(gp.iota(more_no[:, :], [[1, MORE]], 1, 0, **small))
            c(gp.memset(tab_pos[:, :], -BIG))
            c(gp.memset(tab_gate[:, :], 0.0))
            c(gp.memset(st[:, :, :], 1.0))
            assert made[0] == N_CONST, made[0]

            def load_S(b):
                gp.dma_start(Ss[:, b % 3], ins["state_gla_S"][0, b].rearrange("h k v -> k h v")).then_inc(S_loaded[b % 3], 16)

            def mixer_lo(g):
                for n in range(N_QKV):
                    raw, hi, lo = split_parts(g, n)
                    gp.wait_ge(fhi_ready, PART_BEFORE[g] + n + 1)
                    gp.tensor_tensor(lo, raw, hi.bitcast(F32), ALU.subtract).then_inc(mlo_ready, 1)
                gp.wait_ge(*full(f"L{g // 2}v{D // COLS - 1}{TT - 1}"))
                gp.memset(kz[:, :, :], 0.0).then_inc(kz_zero, 1)

            mixer_lo(0)
            for b in range(3):
                load_S(b)
            gp.wait_ge(*copied(f"L0up{NC - 1}a"))
            gp.wait_ge(*copied(f"L0up{NC - 1}b"))
            gp.dma_start(S_p[0, 0].rearrange("h k v -> k h v"), S0[:, 0]).then_inc(prompt_S_stored, 16)
            for b in range(NB):
                gp.wait_ge(*copied(f"L0us{b}a"))
                gp.wait_ge(*copied(f"L0us{b}b"))
                gp.dma_start(S_s[0, b].rearrange("h k v -> k h v"), Ss[:, b % 3]).then_inc(S_stored[b % 3], 16)
                if b + 3 < NB:
                    gp.wait_ge(S_stored[b % 3], 16 * (b // 3 + 1))
                    load_S(b + 3)
            for i in range(3):
                gp.wait_ge(S_stored[i], 16 * S_LOADS[i])
            gp.wait_ge(prompt_S_stored, 16)

            def load_C(b):
                for a in range(2):
                    gp.dma_start(Cs[64 * a:64 * a + 64, b % 3], by_half(ins["state_mlstm_C"][0, b], a))\
                        .then_inc(S_loaded[b % 3], 16)

            gp.wait_ge(*full("Fw7"))
            gp.memset(area(0, 2 * MH * T), 0.0).then_inc(qz_zero, 1)
            mixer_lo(2)
            for b in range(3):
                load_C(b)
            gp.wait_ge(*copied(f"L1up{NC - 1}a"))
            gp.wait_ge(*copied(f"L1up{NC - 1}b"))
            for a in range(2):
                gp.dma_start(by_half(C_p[0, 0], a), C1[64 * a:64 * a + 64, 0]).then_inc(prompt_C_stored, 16)
            for b in range(NB):
                gp.wait_ge(*copied(f"L1us{b}a"))
                gp.wait_ge(*copied(f"L1us{b}b"))
                for a in range(2):
                    gp.dma_start(by_half(C_s[0, b], a), Cs[64 * a:64 * a + 64, b % 3]).then_inc(S_stored[b % 3], 16)
                if b + 3 < NB:
                    gp.wait_ge(S_stored[b % 3], 16 * (S_LOADS[b % 3] + 2 * (b // 3) + 2))
                    load_C(b + 3)
            gp.wait_ge(norm_ready, NC)
            for a in range(2):
                gp.dma_start(n_p[0, 0].rearrange("(j a) k -> a k j", a=2)[a], n_st[64 * a:64 * a + 64, 0], allow_slow_non_contiguous=True).then_inc(small_stored, 16)
            gp.wait_ge(n_new_ready, 1)
            for a in range(2):
                for j in range(4):
                    gp.dma_start(n_s[0].rearrange("b (j a) k -> a j k b", a=2)[a, j], n_new[64 * a:64 * a + 64, j],
                                 allow_slow_non_contiguous=True).then_inc(small_stored, 16)
            gp.dma_start(m_s[0].rearrange("b h -> h b"), m_chunk[:, 1, NC:NC + NB], allow_slow_non_contiguous=True).then_inc(small_stored, 16)
            gp.dma_start(m_p[0, 0].rearrange("(h a) -> h a", a=1), m_chunk[:, 1, NC - 1:NC], allow_slow_non_contiguous=True).then_inc(small_stored, 16)
            gp.wait_ge(small_stored, 16 * 12)
            gp.wait_ge(prompt_C_stored, 32)
            for i in range(3):
                gp.wait_ge(S_stored[i], 16 * 3 * S_LOADS[i])

        @block.tensor
        def _(pe):
            taken = [0]

            def begin(name):
                b, k = uses[name]
                if k:
                    pe.wait_ge(bank_free[b], k)
                return psum[b]

            def end(mm, name):
                mm.then_inc(bank_full[uses[name][0]], 1)

            def weights():
                i = taken[0]
                taken[0] += 1
                s, n = slot(i)
                pe.wait_ge(slot_loaded[n], 16 * (i // RING + 1))
                return s

            pe.wait_ge(const_ready, N_FIRST)
            pe.wait_ge(x_loaded, 48)
            for kt in range(KT):
                bk = begin(f"x{kt}")
                for tt, (t0, n) in enumerate(TS):
                    mm = pe.transpose(bk[:, t0:t0 + n], xtok[0:n, tt, kt * P:(kt + 1) * P], ident[0:n, 0:n])
                end(mm, f"x{kt}")
            pe.wait_ge(par_loaded, 16 * 5)
            bk = begin("par")
            end(pe.transpose(bk[:, 0:52], par_rows[:, :], ident[0:52, 0:52]), "par")

            normed = [None]

            def norm(i, name):
                bk = begin(name)
                for kt in range(KT):
                    pe.wait_ge(sq_ready, KT * i + kt + 1)
                    mm = pe.matmul(bk[:, 0:T], ones[:, :], hT[:, kt, :], start=(kt == 0), stop=(kt == KT - 1))
                end(mm, name)
                normed[0] = i

            def rows_of(bk, w, src, c, n, m):
                for kt in range(n):
                    if normed[0] is not None:
                        pe.wait_ge(h_ready, KT * normed[0] + kt + 1)
                    mm = pe.matmul(bk[0:m, 0:T], w[:, kt, c:c + m], src[:, kt, :], start=(kt == 0), stop=(kt == n - 1))
                normed[0] = None
                return mm

            def three(out, w_hi_, w_lo_, x_hi, x_lo, first, last):
                pe.matmul(out, w_hi_, x_hi, start=first, stop=False, skip_group_check=True)
                pe.matmul(out, w_hi_, x_lo, start=False, stop=False, skip_group_check=True)
                return pe.matmul(out, w_lo_, x_hi, start=False, stop=last, skip_group_check=True)

            def split_weights(g, k):
                n = taken[0] - PART_AT[g]
                taken[0] += 1
                if g == 1:
                    pe.wait_ge(flo_ready, n + 1)
                else:
                    pe.wait_ge(mlo_ready, N_QKV * (g // 2) + n + 1)
                return [w.rearrange("p (k n) -> p k n", k=k) for w in split_parts(g, n)[1:]]

            def tiles(names, src, n=KT):
                w = weights().rearrange("p (k n) -> p k n", k=n)
                for m, name in enumerate(names):
                    bk = begin(name)
                    end(rows_of(bk, w, src, m * P, n, P), name)

            def mixer_qk(l, which):
                g = 2 * int(l[1])
                pe.wait_ge(hlo_ready, KT * (g + 1))
                for m in range(4):
                    if m % 2 == 0:
                        hi, lo = split_weights(g, KT)
                    bk = begin(f"{l}{which}{m}")
                    o = slice(m % 2 * P, (m % 2 + 1) * P)
                    for kt in range(KT):
                        mm = three(bk[:, 0:T], hi[:, kt, o], lo[:, kt, o], mh_hi[:, kt, :], mh_lo[:, kt, :],
                                   kt == 0, kt == KT - 1)
                    end(mm, f"{l}{which}{m}")

            def values(l):
                for s in range(D // COLS):
                    hi, lo = split_weights(2 * int(l[1]), KT)
                    for tt, (t0, n) in enumerate(TS):
                        name = f"{l}v{s}{tt}"
                        bk = begin(name)
                        for kt in range(KT):
                            mm = three(bk[0:n, 0:COLS], mh_hi[:, kt, t0:t0 + n], mh_lo[:, kt, t0:t0 + n], hi[:, kt, :], lo[:, kt, :],
                                       kt == 0, kt == KT - 1)
                        end(mm, name)

            def values_ready(l):
                for tt in range(TT):
                    pe.wait_ge(*copied(f"{l}v{D // COLS - 1}{tt}"))

            def r_pair(l, m):
                tiles([f"{l}r{m}", f"{l}r{m + 1}"], hT)

            def out_proj(l, src, n_before):
                w = weights().rearrange("p (k n) -> p k n", k=KT)
                banks = [begin(f"{l}w{m}") for m in range(2)]
                for kt in range(KT):
                    pe.wait_ge(gated_ready, n_before + kt + 1)
                    for m in range(2):
                        mm = pe.matmul(banks[m][:, 0:T], w[:, kt, m * P:(m + 1) * P], src[:, kt, :],
                                       start=(kt == 0), stop=(kt == KT - 1))
                        if kt == KT - 1:
                            end(mm, f"{l}w{m}")
                for m in range(2, 8, 2):
                    tiles([f"{l}w{m}", f"{l}w{m + 1}"], src)

            norm(0, "L0ss")
            pe.wait_ge(const_ready, N_CONST)
            pe.wait_ge(small_loaded, N_SMALL)
            bk = begin("L0lr")
            end(rows_of(bk, w_lr, hT, 0, KT, RANK), "L0lr")
            mixer_qk("L0", "q")
            pe.wait_ge(*copied("L0lr"))
            for m in range(4):
                bk = begin(f"L0z{m}")
                end(pe.matmul(bk[:, 0:T], w_a2[:, m * P:(m + 1) * P], lr_sb[:, :], start=True, stop=True), f"L0z{m}")
            mixer_qk("L0", "k")
            values("L0")

            pe.wait_ge(kend_ready, 1)
            for tt, (t0, n) in enumerate(TS):
                bk = begin(f"L0kt{tt}")
                for h in range(GH):
                    mm = pe.transpose(bk[0:n, h * P:(h + 1) * P], kend[:, h, t0:t0 + n], ident[:, :])
                end(mm, f"L0kt{tt}")
            pe.wait_ge(qg_ready, 2)
            for tt, (t0, n) in enumerate(TS):
                if tt == 1:
                    r_pair("L0", 0)
                bk = begin(f"L0sc{tt}")
                for h in range(GH):
                    mm = pe.matmul(bk[0:n, h * n:(h + 1) * n], k0[:, h, t0:t0 + n], q0[:, h, t0:t0 + n], start=True, stop=True)
                end(mm, f"L0sc{tt}")

            def update(l, c):
                for half, x in enumerate("ab"):
                    name = f"{l}up{c}{x}"
                    bk = begin(name)
                    for h in range(2):
                        g = 2 * half + h
                        mm = pe.matmul(bk[:, h * 256:(h + 1) * 256], kz[:, c, g * P:(g + 1) * P],
                                       v_tok[:, c // 2, g * 256:(g + 1) * 256], start=True, stop=True)
                    end(mm, name)

            def update_sample(l, b, n_before):
                pe.wait_ge(kb_ready, n_before + b + 1)
                for half, x in enumerate("ab"):
                    name = f"{l}us{b}{x}"
                    bk = begin(name)
                    for h in range(2):
                        g = 2 * half + h
                        mm = pe.matmul(bk[:, h * 256:(h + 1) * 256], kb[:, b % 2, g * P:(g + 1) * P],
                                       v_tok[0:NSM, 2, g * 256:(g + 1) * 256], start=True, stop=True)
                    end(mm, name)

            def own_part(tt, n, scores, names):
                per = 8 // len(names)
                for half, name in enumerate(names):
                    bk = begin(name)
                    for m in range(per):
                        g = per * half + m
                        pe.matmul(bk[:, m * n:(m + 1) * n], v_tok[0:n, tt, g * P:(g + 1) * P], scores(g),
                                  start=(m == 0), stop=False, skip_group_check=True)

            def state_part(l, c, state, query, done):
                pe.wait_ge(*copied(f"{l}up{c - 1}a"))
                pe.wait_ge(*copied(f"{l}up{c - 1}b"))
                for half, x in enumerate("ab"):
                    name = f"{l}o{c // 2}{x}"
                    bk = psum[uses[name][0]]
                    for m in range(4):
                        g = 4 * half + m
                        o = m * P + (c % 2) * L
                        mm = pe.matmul(bk[:, o:o + L], state(g), query(g), start=False, stop=True, skip_group_check=True)
                    if done:
                        end(mm, name)

            def inter0(c, done):
                state_part("L0", c, lambda g: S0[:, c % 2, g // 2, (g % 2) * P:(g % 2 + 1) * P],
                           lambda g: q0[:, g // 2, c * L:(c + 1) * L], done)

            for tt in range(TT):
                pe.wait_ge(*copied(f"L0kt{tt}"))
            values_ready("L0")
            update("L0", 0)
            r_pair("L0", 2)
            update("L0", 1)
            pe.wait_ge(*copied("L0sc0"))
            own_part(0, P, lambda g: P0[:, 0, g // 2, :], ["L0o0a", "L0o0b"])
            inter0(1, True)
            update("L0", 2)
            r_pair("L0", 4)
            pe.wait_ge(*copied("L0sc1"))
            own_part(1, P, lambda g: P0[:, 1, g // 2, :], ["L0o1a", "L0o1b"])
            inter0(2, False)
            update("L0", 3)
            r_pair("L0", 6)
            inter0(3, True)
            pe.wait_ge(*copied("L0sc2"))
            own_part(2, NSM, lambda g: P0s[:, g // 2, :], ["L0o2"])
            for b in range(NB):
                pe.wait_ge(S_loaded[b % 3], 16 * (b // 3 + 1))
                bk = psum[uses["L0o2"][0]]
                for g in range(8):
                    o = g * NSM + b * NS
                    mm = pe.matmul(bk[:, o:o + NS], Ss[:, b % 3, g // 2, (g % 2) * P:(g % 2 + 1) * P],
                                   q0[:, g // 2, NP_ + b * NS:NP_ + (b + 1) * NS], start=False, stop=True, skip_group_check=True)
                if b == NB - 1:
                    end(mm, "L0o2")
                update_sample("L0", b, 0)

            bk = begin("L0ns")
            for g in range(8):
                pe.wait_ge(osq_ready, g // 2 + 1)
                mm = pe.matmul(bk[0:MH, 0:T], head_col[:, g // 2, :], sq0[:, g, :], start=(g == 0), stop=(g == 7))
            end(mm, "L0ns")
            pe.wait_ge(f_ready, 1)
            for h in range(GH):
                bk = begin(f"L0nb{h}")
                end(pe.matmul(bk[:, 0:T], head_row[:, h, :], rows[:, 0, :], start=True, stop=True), f"L0nb{h}")
            out_proj("L0", o0, 0)

            norm(1, "Fss")
            normed[0] = None
            for c in range(FBLK):
                for x in "gu":
                    hi, lo = split_weights(1, KT)
                    for m in range(2):
                        name = f"F{x}{2 * c + m}"
                        bk = begin(name)
                        for kt in range(KT):
                            if c == 0 and x == "g" and m == 0:
                                pe.wait_ge(hlo_ready, KT + kt + 1)
                            o = slice(m * P, (m + 1) * P)
                            mm = three(bk[:, 0:T], hi[:, kt, o], lo[:, kt, o], h_hi[:, kt, :], h_lo[:, kt, :],
                                       kt == 0, kt == KT - 1)
                        end(mm, name)
            pe.wait_ge(ffa_ready, FFT)
            for c in range(D // COLS):
                banks = [begin(f"Fw{2 * c + m}") for m in range(2)]
                for g, (f0, k) in enumerate(DG):
                    hi, lo = split_weights(1, k)
                    for m in range(2):
                        o = slice(m * P, (m + 1) * P)
                        for f in range(k):
                            mm = three(banks[m][:, 0:T], hi[:, f, o], lo[:, f, o], ffa_hi[:, f0 + f, :], ffa_lo[:, f0 + f, :],
                                       f0 + f == 0, f0 + f == FFT - 1)
                        if g == 2:
                            end(mm, f"Fw{2 * c + m}")
                    if g < 2:
                        mm.then_inc(part_used, 1)

            norm(2, "L1ss")
            for a, name in enumerate(("L1gi", "L1gf")):
                bk = begin(name)
                end(rows_of(bk, w_gate, hT, MH * a, KT, MH), name)
            mixer_qk("L1", "q")
            mixer_qk("L1", "k")
            values("L1")

            pe.wait_ge(mexp_ready, 1)
            bk = begin("L1at")
            for tt, (t0, n) in enumerate(TS):
                for a, r in enumerate((2, 7)):
                    c = (2 * tt + a) * MH
                    mm = pe.transpose(bk[0:n, c:c + MH], rows[:, r, t0:t0 + n], ident[0:MH, 0:MH])
            end(mm, "L1at")
            for j in range(4):
                bk = begin(f"L1wb{j}")
                end(pe.matmul(bk[:, 0:T], pair_row[:, j, :], rows[:, 5, :], start=True, stop=True), f"L1wb{j}")
            for m in range(4):
                pe.wait_ge(*copied(f"L1k{m}"))
            for tt, (t0, n) in enumerate(TS):
                bk = begin(f"L1kt{tt}")
                for j in range(4):
                    mm = pe.transpose(bk[0:n, j * P:(j + 1) * P], k1[:, j, t0:t0 + n], ident[:, :])
                end(mm, f"L1kt{tt}")

            def decay_and_scores(tt, t0, n, parts, halves):
                per = MH // halves
                for kind in ("db", "sc"):
                    for hf in range(halves):
                        name = f"L1{kind}{tt}{parts[hf]}"
                        bk = begin(name)
                        for h in range(per):
                            g = per * hf + h
                            if kind == "db":
                                mm = pe.matmul(bk[0:n, h * n:(h + 1) * n], head_row[:, g, 0:n], rows[:, 4, t0:t0 + n], start=True, stop=True)
                            else:
                                mm = pe.matmul(bk[0:n, h * n:(h + 1) * n], k1[:, g // 2, t0:t0 + n], qz[:, g, t0:t0 + n], start=True, stop=True)
                        end(mm, name)

            decay_and_scores(0, 0, P, "01", 2)
            r_pair("L1", 0)
            for tt in range(TT):
                pe.wait_ge(*copied(f"L1kt{tt}"))
            bk = begin("L1nu")
            for j in range(4):
                for c in range(NC):
                    pe.matmul(bk[:, j * 12 + c:j * 12 + c + 1], kz[:, c, j * P:(j + 1) * P], ones[:, 0:1], start=True, stop=True)
                mm = pe.matmul(bk[:, j * 12 + NC:(j + 1) * 12], kz[0:NSM, NC, j * P:(j + 1) * P], batch_of[:, :], start=True, stop=True)
            end(mm, "L1nu")
            decay_and_scores(1, P, P, "01", 2)
            r_pair("L1", 2)
            decay_and_scores(2, NP_, NSM, [""], 1)

            den = psum[uses["L1den"][0]]

            def den_own(tt, t0, n, Pm):
                for g in range(MH):
                    pe.matmul(den[0:MH, t0:t0 + n], head_col[0:n, g, :], Pm[:, g, :], start=(tt == 0 and g == 0),
                              stop=False, skip_group_check=True)

            def inter1(c, done):
                pe.wait_ge(norm_ready, c)
                for g in range(MH):
                    pe.matmul(den[0:MH, c * L:(c + 1) * L], n_cols[:, c % 2, g, :], qwz[:, g, c * L:(c + 1) * L],
                              start=False, stop=True, skip_group_check=True)
                state_part("L1", c, lambda g: C1[:, c % 2, g // 2, :], lambda g: qwz[:, g, c * L:(c + 1) * L], done)

            values_ready("L1")
            update("L1", 0)
            update("L1", 1)
            r_pair("L1", 4)
            pe.wait_ge(*copied("L1sc00"))
            pe.wait_ge(*copied("L1sc01"))
            own_part(0, P, lambda g: P1[:, 0, g, :], ["L1o0a", "L1o0b"])
            begin("L1den")
            den_own(0, 0, P, P1[:, 0])
            inter1(1, True)
            update("L1", 2)
            pe.wait_ge(*copied("L1sc10"))
            pe.wait_ge(*copied("L1sc11"))
            own_part(1, P, lambda g: P1[:, 1, g, :], ["L1o1a", "L1o1b"])
            den_own(1, P, P, P1[:, 1])
            inter1(2, False)
            update("L1", 3)
            r_pair("L1", 6)
            inter1(3, True)
            pe.wait_ge(*copied("L1sc2"))
            own_part(2, NSM, lambda g: P1s[:, g, :], ["L1o2"])
            den_own(2, NP_, NSM, P1s)
            pe.wait_ge(norm_ready, NC + 1)
            for g in range(MH):
                mm = pe.matmul(den[0:MH, NP_:T], head_col[:, g, :], qn[:, g, :], start=False, stop=True, skip_group_check=True)
            end(mm, "L1den")
            for b in range(NB):
                pe.wait_ge(S_loaded[b % 3], 16 * (S_LOADS[b % 3] + 2 * (b // 3) + 2))
                bk = psum[uses["L1o2"][0]]
                for g in range(MH):
                    o = g * NSM + b * NS
                    mm = pe.matmul(bk[:, o:o + NS], Cs[:, b % 3, g // 2, :], qwz[:, g, NP_ + b * NS:NP_ + (b + 1) * NS],
                                   start=False, stop=True, skip_group_check=True)
                if b == NB - 1:
                    end(mm, "L1o2")
                update_sample("L1", b, NB)
            bk = begin("L1ns")
            for g in range(MH):
                pe.wait_ge(osq_ready, GH + g + 1)
                mm = pe.matmul(bk[0:MH, 0:T], head_col[:, g, :], sq1[:, g, :], start=(g == 0), stop=(g == 7))
            end(mm, "L1ns")
            pe.wait_ge(f_ready, 2)
            for h in range(MH):
                bk = begin(f"L1nb{h}")
                end(pe.matmul(bk[:, 0:T], head_row[:, h, :], rows[:, 0, :], start=True, stop=True), f"L1nb{h}")
            out_proj("L1", num, 8)

            norm(3, "Mss")
            bk = begin("Mlog")
            for tt, (t0, n) in enumerate(TS):
                for kt in range(KT):
                    if tt == 0:
                        pe.wait_ge(h_ready, 3 * KT + kt + 1)
                    mm = pe.matmul(bk[0:n, tt * NE:(tt + 1) * NE], hT[:, kt, t0:t0 + n], w_rt[:, kt, :],
                                   start=(kt == 0), stop=(kt == KT - 1))
                if tt == 0:
                    mm.then_inc(split_used, 1)
            end(mm, "Mlog")
            for c, src in (("h", hT), ("x", xT)):
                for kt in range(KT):
                    bk = begin(f"M{c}{kt}")
                    for tt, (t0, n) in enumerate(TS):
                        mm = pe.transpose(bk[0:n, tt * P:(tt + 1) * P], src[:, kt, t0:t0 + n], ident[:, :])
                    end(mm, f"M{c}{kt}")
            pe.wait_ge(chosen_ready, 1)
            bk = begin("Mrank")
            for tt in range(TT):
                for s in range(tt + 1):
                    pe.matmul(bk[:, tt * NE:(tt + 1) * NE], (before if s == tt else ones)[:, :], chosen[:, s, :],
                              start=(s == 0), stop=(s == tt))
            for s in range(TT):
                mm = pe.matmul(bk[:, TT * NE:(TT + 1) * NE], ones[:, :], chosen[:, s, :], start=(s == 0), stop=(s == TT - 1))
            end(mm, "Mrank")

            def gather(bank_of):
                for half in range(2):
                    b = bank_of(half)
                    for m in range(4):
                        kt = 4 * half + m
                        for tt in range(TT):
                            mm = pe.matmul(psum[b][:, m * CAP:(m + 1) * CAP], h_tok[:, tt, kt * P:(kt + 1) * P], sel[:, tt, :],
                                           start=(tt == 0), stop=(tt == TT - 1))
                    mm.then_inc(bank_full[b], 1)

            def first_bank(half):
                begin(f"Mga{half}")
                return uses[f"Mga{half}"][0]

            for kt in range(KT):
                pe.wait_ge(*copied(f"Mh{kt}"))
            pe.wait_ge(sel_ready, 1)
            gather(first_bank)
            pe.wait_ge(table_ready, 1)
            n_items = pe.value_load(tab_i[0:1, 15:16], min_val=NE, max_val=NE + MORE)

            def scatter(n, i, b, k):
                tt, half = n // 2, n % 2
                pe.wait_ge(*loop_before(b, k, i))
                pe.matmul(psum[b][:, :], selT[:, tt * P:(tt + 1) * P], ye[:, half * 512:(half + 1) * 512],
                          start=True, stop=True).then_inc(bank_full[b], 1)

            def output_read(i):
                for b in YB:
                    pe.wait_ge(bank_free[b], i + (static_turns[b] + 1))

            pe.wait_ge(pad_zero, 1)
            with pe.Fori(0, n_items) as i:
                def parts(kind, nth, x):
                    at = expert_at[kind, nth, x]
                    pe.wait_ge(wlo_ready, i * PER + (at + 1))
                    k = 2 if kind == "d" else HALF
                    return [w[:, at % SPLIT, :].rearrange("p (k n) -> p k n", k=k) for w in (w_hi, w_lo)]

                def project(kind, nth):
                    b = (GB if kind == "g" else UB)[nth % 2]
                    pe.wait_ge(*loop_before(b, nth // 2, i))
                    for x in range(2):
                        hi, lo = parts(kind, nth, x)
                        for m in range(HALF):
                            kt = x * HALF + m
                            mm = three(psum[b][0:CAP, :], xg_hi[:, kt, :], xg_lo[:, kt, :], hi[:, m, :], lo[:, m, :],
                                       kt == 0, kt == KT - 1)
                        mm.then_inc(*((split_used, 1) if x == 0 else (bank_full[b], 1)))

                def turn_act(nth):
                    pe.wait_ge(*loop_before(UB[nth % 2], nth // 2 + 1, i))
                    pe.wait_ge(*loop_before(TB, nth, i))
                    for f in range(4):
                        mm = pe.transpose(psum[TB][:, f * CAP:(f + 1) * CAP], act[:, f * P:(f + 1) * P], ident[0:CAP, 0:CAP])
                    mm.then_inc(bank_full[TB], 1)

                def down(nth):
                    pe.wait_ge(*loop_before(TB, nth + 1, i))
                    if nth == 0:
                        output_read(i)
                    for x in range(2):
                        hi, lo = parts("d", nth, x)
                        for half in range(2):
                            c = slice(half * 512, (half + 1) * 512)
                            for m in range(2):
                                f = 2 * x + m
                                end_ = nth == STEPS - 1 and f == 3
                                mm = three(psum[YB[half]][0:CAP, :], aT_hi[:, f, :], aT_lo[:, f, :], hi[:, m, c], lo[:, m, c],
                                           nth == 0 and f == 0, end_)
                            if end_:
                                mm.then_inc(bank_full[YB[half]], 1)
                        if not end_:
                            mm.then_inc(split_used, 1)

                for b in GAB:
                    pe.wait_ge(*loop_before(b, 0, i))
                project("g", 0)
                project("u", 0)
                for nth in range(1, STEPS):
                    project("g", nth)
                    turn_act(nth - 1)
                    project("u", nth)
                    if nth == 1:
                        output_read(i)
                    scatter(nth - 1, i, MB, nth - 1)
                    down(nth - 1)
                turn_act(STEPS - 1)
                pe.wait_ge(selg_ready, i + 1)
                pe.wait_ge(*loop_before(MB, 6, i))
                for tt in range(TT):
                    mm = pe.transpose(psum[MB][0:CAP, tt * P:(tt + 1) * P], selg[:, tt, :], ident[:, :])
                mm.then_inc(bank_full[MB], 1)
                pe.wait_ge(sel_ready, i + 2)

                def next_bank(half):
                    pe.wait_ge(*loop_before(GAB[half], 3, i))
                    return GAB[half]

                gather(next_bank)
                down(STEPS - 1)
            output_read(n_items)
            for n in range(6):
                scatter(n, n_items, (MB, TB)[n % 2], n // 2)

        @block.scalar
        def _(ac):
            chain = [0]

            def step(ins_):
                chain[0] += 1
                ins_.then_inc(a_chain, 1)
                ac.wait_ge(a_chain, chain[0])

            def take(name):
                b, k = uses[name]
                ac.wait_ge(bank_full[b], k + 1)
                return psum[b]

            def free(ins_, name):
                ins_.then_inc(bank_free[uses[name][0]], 1)

            one, zero = one_col[:, 0:1], one_col[:, 1:2]
            for tt in range(2):
                ac.dma_start(xtok[:, tt, :], ins["x_prompt"][0, tt * P:(tt + 1) * P, :]).then_inc(x_loaded, 16)
            ac.dma_start(xtok[0:NSM, 2, :], ins["x_sample"].rearrange("b t d -> (b t) d")).then_inc(x_loaded, 16)

            def norm(i, name, source, readers):
                if readers:
                    ac.wait_ge(*full(readers))
                for kt in range(KT):
                    ac.wait_ge(*copied(f"{source}{kt}"))
                    ac.activation(hT[:, kt, :], xT[:, kt, :], ACT.Square, bias=zero).then_inc(sq_ready, 1)
                ac.wait_ge(*copied(name))
                ac.activation(rbc[:, 1, :], rbc[:, 0, :], ACT.Abs_reciprocal_sqrt, bias=zero).then_inc(inv_ready, 1)

            def first_bits(g, n):
                raw, hi, _ = split_parts(g, n)
                i = PART_AT[g] + n
                ac.wait_ge(slot_loaded[i % RING], 16 * (i // RING + 1))
                if n >= HI_SLOTS:
                    ac.wait_ge(*static_loads[i - HI_SLOTS][1])
                ac.activation(hi, raw, ACT.Copy).then_inc(fhi_ready, 1)

            def input_hi(i, dst):
                for kt in range(KT):
                    ac.wait_ge(h_ready, KT * i + kt + 1)
                    ac.activation(dst[:, kt, :], hT[:, kt, :], ACT.Copy).then_inc(hhi_ready, 1)

            def head_norm(n):
                ac.wait_ge(mean_ready, n)
                ac.activation(rows[:, 1, :], rows[:, 0, :], ACT.Abs_reciprocal_sqrt, bias=zero[0:MH]).then_inc(rowx_ready, 1)

            def values(l):
                for s in range(D // COLS):
                    for tt, (t0, n) in enumerate(TS):
                        name = f"{l}v{s}{tt}"
                        free(ac.activation(v_tok[0:n, tt, s * COLS:(s + 1) * COLS], take(name)[0:n, 0:COLS], ACT.Copy), name)
                    if s == 0:
                        first_bits(2 * int(l[1]), 7)

            def gate(l, m, func):
                free(ac.activation(gate_r[:, m, :], take(f"{l}r{m}")[:, 0:T], func, bias=zero), f"{l}r{m}")

            def output(l, o, tt):
                if tt < 2:
                    for half, x in enumerate("ab"):
                        name = f"{l}o{tt}{x}"
                        free(ac.activation(o[:, 4 * half:4 * half + 4, tt * P:(tt + 1) * P],
                                           take(name)[:, :].rearrange("p (g t) -> p g t", g=4), ACT.Copy), name)
                else:
                    name = l + "o2"
                    free(ac.activation(o[:, :, NP_:T], take(name)[:, 0:8 * NSM].rearrange("p (g t) -> p g t", g=8), ACT.Copy), name)

            ac.wait_ge(const_ready, N_FIRST)
            norm(0, "L0ss", "x", None)
            first_bits(0, 0)
            first_bits(0, 1)
            input_hi(0, mh_hi)
            first_bits(0, 2)
            ac.wait_ge(const_ready, N_CONST)
            free(ac.activation(lr_sb[:, :], take("L0lr")[0:RANK, 0:T], ACT.Copy), "L0lr")
            for m in range(4):
                free(ac.activation(q0[:, m, :], take(f"L0q{m}")[:, 0:T], ACT.Copy), f"L0q{m}")
                if m % 2:
                    first_bits(0, 3 + m // 2)
            for h in range(4):
                ac.wait_ge(abs_ready, h + 1)
                step(ac.activation(t2[:, h, :], t2[:, h, :], ACT.Exp, bias=zero, scale=-1.0))
            for h in range(4):
                ac.activation(t2[:, h, :], t2[:, h, :], ACT.Ln, bias=one).then_inc(ln_ready, 1)
            for m in range(4):
                free(ac.activation(k0[:, m, :], take(f"L0k{m}")[:, 0:T], ACT.Copy, scale=float(P) ** -0.5), f"L0k{m}")
                if m % 2:
                    first_bits(0, 5 + m // 2)
            ac.wait_ge(cum_ready, 6)
            ac.activation(t1[:, :, :], cum[:, :, :], ACT.Exp, bias=zero, scale=1 / TAU).then_inc(dec_ready, 1)
            ac.activation(t2[:, :, :], t2[:, :, :], ACT.Exp, bias=zero, scale=1 / TAU).then_inc(dec_ready, 1)
            ac.activation(eb[:, :, 0:NC], cum[:, :, L - 1:NP_:L], ACT.Exp, bias=zero, scale=1 / TAU).then_inc(dec_ready, 1)
            ac.activation(eb[:, :, NC:NC + NB], cum[:, :, NP_ + NS - 1:T:NS], ACT.Exp, bias=zero, scale=1 / TAU).then_inc(dec_ready, 1)
            ac.wait_ge(qg_ready, 1)
            ac.activation(t1[:, :, :], cum[:, :, :], ACT.Exp, bias=zero, scale=-1 / TAU).then_inc(dec_ready, 1)
            values("L0")
            for m in range(4):
                gate("L0", m, ACT.Silu)
            ac.wait_ge(qg_ready, 2)
            output("L0", o0, 0)
            for m in range(4, 8):
                gate("L0", m, ACT.Silu)
            output("L0", o0, 1)
            output("L0", o0, 2)
            ac.wait_ge(*copied("L0o2"))
            ac.wait_ge(*copied("L0o1b"))
            ac.wait_ge(*full("L0sc2"))
            for h in range(GH):
                ac.activation(sq0[:, 2 * h:2 * h + 2, :], o0[:, 2 * h:2 * h + 2, :], ACT.Square, bias=zero).then_inc(osq_ready, 1)
            head_norm(1)

            ac.wait_ge(gated_ready, 8)
            for n in range(HI_SLOTS):
                first_bits(1, n)
            norm(1, "Fss", "L0w", "L0r7")
            for i in range(3):
                ac.wait_ge(S_stored[i], 16 * S_LOADS[i])
            input_hi(1, h_hi)
            for f in range(FFT):
                if f >= 2:
                    ac.wait_ge(*copied(f"Fu{f - 2}"))
                free(ac.activation(ffg[:, f % 2, :], take(f"Fg{f}")[:, 0:T], ACT.Silu, bias=zero), f"Fg{f}")
                if f % 2:
                    first_bits(1, f + 2)
                    first_bits(1, f + 3)
            for n in range(2 * FBLK + HI_SLOTS, N_FFN):
                first_bits(1, n)

            norm(2, "L1ss", "Fw", f"Fu{FFT - 1}")
            first_bits(2, 0)
            first_bits(2, 1)
            input_hi(2, mh_hi)
            first_bits(2, 2)
            ac.wait_ge(*copied("L1gf"))
            for r in range(2):
                ac.activation(rows[:, r, :], rows[:, r, :], ACT.Tanh, bias=zero[0:MH], scale=1 / CAPG).then_inc(tanh_ready, 1)
            ac.wait_ge(qz_zero, 1)

            def q_pair(m):
                bk = take(f"L1q{m}")
                ac.activation(qz[0:64, 2 * m, :], bk[0:64, 0:T], ACT.Copy).then_inc(q_half, 1)
                free(ac.activation(qz[64:128, 2 * m + 1, :], bk[64:128, 0:T], ACT.Copy), f"L1q{m}")

            q_pair(0)
            q_pair(1)
            first_bits(2, 3)
            ac.wait_ge(fabs_ready, 1)
            step(ac.activation(rows[:, 2, :], rows[:, 2, :], ACT.Exp, bias=zero[0:MH], scale=-1.0))
            ac.activation(rows[:, 2, :], rows[:, 2, :], ACT.Ln, bias=one[0:MH]).then_inc(fln_ready, 1)
            q_pair(2)
            q_pair(3)
            first_bits(2, 4)
            for m in range(4):
                free(ac.activation(k1[:, m, :], take(f"L1k{m}")[:, 0:T], ACT.Copy, scale=64.0 ** -0.5), f"L1k{m}")
                if m % 2:
                    first_bits(2, 5 + m // 2)
            ac.wait_ge(mexpo_ready, 1)
            ac.activation(rows[:, 5:8, :], rows[:, 5:8, :], ACT.Exp, bias=zero[0:MH]).then_inc(mexp_ready, 1)
            values("L1")
            for tt, (t0, n) in enumerate(TS):
                ac.wait_ge(dmp_ready, tt + 1)
                v = dmp[0:n, :, 0:n]
                ac.activation(v, v, ACT.Exp, bias=zero[0:n]).then_inc(dexp_ready, 1)
                if tt < 2:
                    for m in (2 * tt, 2 * tt + 1):
                        gate("L1", m, ACT.Sigmoid)
            gate("L1", 4, ACT.Sigmoid)
            gate("L1", 5, ACT.Sigmoid)
            output("L1", num, 0)
            gate("L1", 6, ACT.Sigmoid)
            gate("L1", 7, ACT.Sigmoid)
            output("L1", num, 1)
            output("L1", num, 2)
            ac.wait_ge(*copied("L1o2"))
            ac.wait_ge(*copied("L1o1b"))
            ac.wait_ge(qw_ready, 8)
            for h in range(MH):
                ac.activation(sq1[:, h, :], num[:, h, :], ACT.Square, bias=zero).then_inc(osq_ready, 1)
            head_norm(2)

            norm(3, "Mss", "L1w", "L1r7")
            ac.wait_ge(logit_ready, 1)
            ac.activation(pr[:, :, :], lg[:, :, :], ACT.Exp, bias=zero).then_inc(prob_ready, 1)
            ac.wait_ge(tok_cleared, 1)
            for kt in range(KT):
                bk = take(f"Mh{kt}")
                step(ac.activation(h_tok[:, 0:2, kt * P:(kt + 1) * P], bk[:, 0:2 * P].rearrange("p (a b) -> p a b", a=2), ACT.Copy))
                free(ac.activation(h_tok[0:NSM, 2, kt * P:(kt + 1) * P], bk[0:NSM, 2 * P:3 * P], ACT.Copy), f"Mh{kt}")
            for half in range(2):
                ac.activation(xg_hi[:, 4 * half:4 * half + 4, :],
                              take(f"Mga{half}")[:, 0:4 * CAP].rearrange("p (k c) -> p k c", k=4), ACT.Copy).then_inc(hi_ready, 1)
            ac.wait_ge(table_ready, 1)
            n_items = ac.value_load(tab_i[0:1, 15:16], min_val=NE, max_val=NE + MORE)

            def read_output(i):
                for half in range(2):
                    b = YB[half]
                    ac.wait_ge(bank_full[b], i + static_turns[b])
                    ac.activation(ye[:, half * 512:(half + 1) * 512], psum[b][0:CAP, :], ACT.Copy).then_inc(bank_free[b], 1)

            with ac.Fori(0, n_items) as i:
                for j in range(PER):
                    src, s = expert_slot(j)
                    ac.wait_ge(slot_loaded[s], i * (16 * PER // RING) + 16 * (loads_before(s) + j // RING + 1))
                    split_free(ac, j, i)
                    ac.activation(w_hi[:, j % SPLIT, :], src, ACT.Copy).then_inc(whi_ready, 1)
                    due = expert_order[j - SPLIT] if j >= SPLIT else None
                    if j == SPLIT - 1:
                        ac.wait_ge(*loop_before(MB, 0, i))
                        read_output(i)
                    if due and due[0] == "g" and due[2] == 1:
                        t = due[1]
                        b = GB[t % 2]
                        ac.wait_ge(*loop_full(b, t // 2, i))
                        ac.wait_ge(*loop_before(UB[t % 2], t // 2, i))
                        ac.activation(sg[:, t % 2, :], psum[b][0:CAP, :], ACT.Silu, bias=zero[0:CAP]).then_inc(bank_free[b], 1)
                        if t:
                            turned_hi(ac, t - 1, i)
                turned_hi(ac, STEPS - 1, i)
                for half in range(2):
                    ac.wait_ge(*loop_full(GAB[half], 3, i))
                    ac.activation(xg_hi[:, 4 * half:4 * half + 4, :],
                                  psum[GAB[half]][:, 0:4 * CAP].rearrange("p (k c) -> p k c", k=4), ACT.Copy).then_inc(hi_ready, 1)
            read_output(n_items)

            for b in (MB, TB):
                ac.wait_ge(*loop_before(b, 3, n_items))
            for tt, (t0, n) in enumerate(TS):
                ac.activation(h_tok[0:n, tt, :], x_acc[0:n, tt, :], ACT.Square, bias=zero[0:n],
                              accum_out=st[0:n, 4, tt:tt + 1]).then_inc(fsq_ready, 1)
            ac.wait_ge(fmean_ready, 1)
            ac.activation(st[:, 5, :], st[:, 4, :], ACT.Abs_reciprocal_sqrt, bias=zero).then_inc(finv_ready, 1)
            for tt, (t0, n) in enumerate(TS):
                ac.wait_ge(out_ready, tt + 1)
                dst = y_p[0, t0:t0 + n, :] if tt < 2 else y_s.rearrange("b t d -> (b t) d")
                ac.dma_start(dst, x_acc[0:n, tt, :]).then_inc(out_stored, 16)
            ac.wait_ge(out_stored, 48)

        @block.vector
        def _(ve):
            chain = [0]

            def step(ins_):
                chain[0] += 1
                ins_.then_inc(v_chain, 1)
                ve.wait_ge(v_chain, chain[0])

            def take(name):
                b, k = uses[name]
                ve.wait_ge(bank_full[b], k + 1)
                return psum[b]

            def free(ins_, name):
                ins_.then_inc(bank_free[uses[name][0]], 1)

            def free_step(ins_, name):
                free(ins_, name)
                ve.wait_ge(*copied(name))

            def stt(out, a, s, b, op0, op1):
                return ve.scalar_tensor_tensor(out=out, in0=a, scalar=s, in1=b, op0=op0, op1=op1)

            def polish(x, y, t, last):
                step(stt(t, x, -0.5, y, ALU.mult, ALU.mult))
                step(ve.tensor_tensor(t, t, y, ALU.mult))
                last(stt(y, t, 1.5, y, ALU.add, ALU.mult))

            def input_lo(i, hi, lo, kt):
                ve.wait_ge(hhi_ready, KT * i + kt + 1)
                ve.tensor_tensor(lo[:, kt, :], hT[:, kt, :], hi[:, kt, :].bitcast(F32), ALU.subtract).then_inc(hlo_ready, 1)

            def norm(i, name, split=None):
                free(ve.tensor_scalar(rbc[:, 0, :], take(name)[:, 0:T], 1.0 / D, EPS, ALU.mult, ALU.add), name)
                ve.wait_ge(inv_ready, i + 1)
                polish(rbc[:, 0, :], rbc[:, 1, :], rbc[:, 0, :], step)
                g0 = [0, 16, 8, 24][i]
                for kt in range(KT):
                    stt(hT[:, kt, :], xT[:, kt, :], par[:, g0 + kt:g0 + kt + 1], rbc[:, 1, :], ALU.mult, ALU.mult)\
                        .then_inc(h_ready, 1)
                    if split and kt:
                        input_lo(i, *split, kt - 1)
                if split:
                    input_lo(i, *split, KT - 1)

            def residual(prefix, tiles_):
                for m in tiles_:
                    name = f"{prefix}{m}"
                    free(ve.tensor_tensor(xT[:, m, :], xT[:, m, :], take(name)[:, 0:T], ALU.add), name)

            def over_heads(m, n):
                p = m.shape[0]
                return m.unsqueeze(1).broadcast_to([p, n, m.shape[1]])

            def sample_keys(l, b, n_before):
                if b >= 2:
                    ve.wait_ge(*full(f"{l}us{b - 2}b"))
                ve.tensor_scalar(kb[:, b % 2, :], kz[0:NSM, NC, :], batch_of[:, b:b + 1], None, ALU.mult).then_inc(kb_ready, 1)

            def gated(l, o, heads, tiles_, g0):
                for h in range(heads):
                    bk = take(f"{l}nb{h}")
                    for a in range(tiles_):
                        g = tiles_ * h + a
                        ins_ = stt(o[:, g, :], o[:, g, :], par[:, g0 + g:g0 + g + 1], bk[:, 0:T], ALU.mult, ALU.mult)
                    free_step(ins_, f"{l}nb{h}")
                    for a in range(tiles_):
                        g = tiles_ * h + a
                        ve.wait_ge(*copied(f"{l}r{g}"))
                        ve.tensor_tensor(o[:, g, :], o[:, g, :], gate_r[:, g, :], ALU.mult).then_inc(gated_ready, 1)

            for kt in range(KT):
                free(ve.tensor_copy(xT[:, kt, :], take(f"x{kt}")[:, 0:T]), f"x{kt}")
            free_step(ve.tensor_copy(par[:, :], take("par")[:, 0:52]), "par")

            norm(0, "L0ss", (mh_hi, mh_lo))
            ve.wait_ge(const_ready, N_CONST)
            ve.wait_ge(small_loaded, N_SMALL)
            for h in range(4):
                free_step(ve.tensor_scalar(t1[:, h, :], take(f"L0z{h}")[:, 0:T], par[:, 32 + h:33 + h], None, ALU.add), f"L0z{h}")
                stt(t2[:, h, :], t1[:, h, :], -1.0, t1[:, h, :], ALU.mult, ALU.max).then_inc(abs_ready, 1)
            for h in range(4):
                ve.wait_ge(ln_ready, h + 1)
                step(stt(t1[:, h, :], t1[:, h, :], 0.0, t2[:, h, :], ALU.min, ALU.subtract))
                ve.tensor_tensor_scan(cum[:, h, :], going[:, :], t1[:, h, :], 0.0, ALU.mult, ALU.add).then_inc(cum_ready, 1)
            ve.wait_ge(cum_ready, 4)

            def chunks(t):
                a, n, _ = t.shape
                return ((t[:, :, 0:NP_].rearrange("p h (c t) -> p h c t", c=NC),
                         t[:, :, L - 1:NP_:L].unsqueeze(3).broadcast_to([a, n, NC, L])),
                        (t[:, :, NP_:T].rearrange("p h (c t) -> p h c t", c=NB),
                         t[:, :, NP_ + NS - 1:T:NS].unsqueeze(3).broadcast_to([a, n, NB, NS])))

            for (out, _), (x, last) in zip(chunks(t2), chunks(cum)):
                ve.tensor_tensor(out, last, x, ALU.subtract).then_inc(cum_ready, 1)
            for m in range(4):
                ve.wait_ge(*copied(f"L0q{m}"))
            ve.wait_ge(dec_ready, 1)
            ve.tensor_tensor(q0[:, :, :], q0[:, :, :], t1[:, :, :], ALU.mult).then_inc(qg_ready, 1)
            for m in range(4):
                ve.wait_ge(*copied(f"L0k{m}"))
            ve.wait_ge(dec_ready, 2)
            ve.tensor_tensor(kend[:, :, :], k0[:, :, :], t2[:, :, :], ALU.mult).then_inc(kend_ready, 1)
            ve.wait_ge(dec_ready, 5)
            ve.tensor_tensor(k0[:, :, :], k0[:, :, :], t1[:, :, :], ALU.mult).then_inc(qg_ready, 1)
            ve.wait_ge(kz_zero, 1)
            for tt in range(2):
                bk = take(f"L0kt{tt}")
                ve.tensor_copy(kz[0:64, 2 * tt, :], bk[0:64, :])
                free(ve.tensor_copy(kz[64:128, 2 * tt + 1, :], bk[64:128, :]), f"L0kt{tt}")
            free_step(ve.tensor_copy(kz[0:NSM, NC, :], take("L0kt2")[0:NSM, :]), "L0kt2")
            for tt in range(TT):
                n = TS[tt][1]
                out, m = (P0[:, tt], causal) if tt < 2 else (P0s, causal_s)
                free(ve.tensor_tensor(out, take(f"L0sc{tt}")[0:n, 0:GH * n].rearrange("p (h t) -> p h t", h=GH),
                                      over_heads(m[:, :], GH), ALU.mult), f"L0sc{tt}")
            sample_keys("L0", 0, 0)
            sample_keys("L0", 1, 0)
            for c in range(NC):
                for half, x in enumerate("ab"):
                    name = f"L0up{c}{x}"
                    bk = take(name)
                    if c == 0:
                        free_step(ve.tensor_copy(S0[:, 1, 2 * half:2 * half + 2, :], bk[:, :].rearrange("p (h v) -> p h v", h=2)), name)
                        continue
                    for a in range(2):
                        h = 2 * half + a
                        ins_ = stt(S0[:, (c + 1) % 2, h, :], S0[:, c % 2, h, :], eb[:, h, c:c + 1], bk[:, a * 256:(a + 1) * 256],
                                   ALU.mult, ALU.add)
                    free_step(ins_, name)
            for b in range(NB):
                ve.wait_ge(S_loaded[b % 3], 16 * (b // 3 + 1))
                for half, x in enumerate("ab"):
                    name = f"L0us{b}{x}"
                    bk = take(name)
                    for a in range(2):
                        h = 2 * half + a
                        ins_ = stt(Ss[:, b % 3, h, :], Ss[:, b % 3, h, :], eb[:, h, NC + b:NC + b + 1], bk[:, a * 256:(a + 1) * 256],
                                   ALU.mult, ALU.add)
                    free(ins_, name)
                if b + 2 < NB:
                    sample_keys("L0", b + 2, 0)
            ve.tensor_scalar(rows[:, 0, :], take("L0ns")[0:MH, 0:T], 1.0 / GDV, EPS, ALU.mult, ALU.add).then_inc(mean_ready, 1)
            ve.wait_ge(mean_ready, 1)
            ve.wait_ge(rowx_ready, 1)
            step(stt(rows[:, 2, :], rows[:, 0, :], -0.5, rows[:, 1, :], ALU.mult, ALU.mult))
            step(ve.tensor_tensor(rows[:, 2, :], rows[:, 2, :], rows[:, 1, :], ALU.mult))
            stt(rows[:, 0, :], rows[:, 2, :], 1.5, rows[:, 1, :], ALU.add, ALU.mult).then_inc(f_ready, 1)
            ve.tensor_copy(m_chunk[:, 2, 0:1], rows[:, 2, 0:1]).then_inc(bank_free[uses["L0ns"][0]], 1)
            gated("L0", o0, GH, 2, 36)

            def last_bits(n):
                raw, hi, lo = split_parts(1, n)
                ve.wait_ge(fhi_ready, PART_BEFORE[1] + n + 1)
                ve.tensor_tensor(lo, raw, hi.bitcast(F32), ALU.subtract).then_inc(flo_ready, 1)

            for n in range(HI_SLOTS):
                last_bits(n)
            residual("L0w", range(KT))
            norm(1, "Fss", (h_hi, h_lo))
            ve.wait_ge(prompt_S_stored, 16)
            for f in range(FFT):
                if f % 2 == 0:
                    last_bits(f + 3)
                ve.wait_ge(*copied(f"Fg{f}"))
                free_step(ve.tensor_tensor(ffp[:, f % 2, :], ffg[:, f % 2, :], take(f"Fu{f}")[:, 0:T], ALU.mult), f"Fu{f}")
                step(ve.tensor_copy(ffa_hi[:, f, :], ffp[:, f % 2, :]))
                ve.tensor_tensor(ffa_lo[:, f, :], ffp[:, f % 2, :], ffa_hi[:, f, :].bitcast(F32), ALU.subtract).then_inc(ffa_ready, 1)
                if f % 2:
                    last_bits(f + 3)
            for c in range(D // COLS):
                for g in range(len(DG)):
                    n = 2 * FBLK + len(DG) * (c + 1) + g
                    if n < N_FFN:
                        last_bits(n)
                residual("Fw", (2 * c, 2 * c + 1))

            norm(2, "L1ss", (mh_hi, mh_lo))
            free(ve.tensor_scalar(rows[:, 0, :], take("L1gi")[0:MH, 0:T], b_i[:, 0:1], None, ALU.add), "L1gi")
            free(ve.tensor_scalar(rows[:, 1, :], take("L1gf")[0:MH, 0:T], b_f[:, 0:1], None, ALU.add), "L1gf")
            ve.wait_ge(tanh_ready, 2)
            step(ve.tensor_scalar(rows[:, 0:2, :], rows[:, 0:2, :], CAPG, None, ALU.mult))
            stt(rows[:, 2, :], rows[:, 1, :], -1.0, rows[:, 1, :], ALU.mult, ALU.max).then_inc(fabs_ready, 1)
            ve.wait_ge(fln_ready, 1)
            step(stt(rows[:, 1, :], rows[:, 1, :], 0.0, rows[:, 2, :], ALU.min, ALU.subtract))
            step(ve.tensor_tensor_scan(rows[:, 3, :], going[0:MH, :], rows[:, 1, :], 0.0, ALU.mult, ALU.add))
            step(ve.tensor_tensor(rows[:, 2, :], rows[:, 0, :], rows[:, 3, :], ALU.subtract))
            step(ve.tensor_tensor_scan(rows[:, 8, :], drop[:, :], rows[:, 2, :], 0.0, ALU.add, ALU.max))

            def last_of(r, prompt):
                return rows[:, r, L - 1:NP_:L] if prompt else rows[:, r, NP_ + NS - 1:T:NS]

            step(ve.memset(m_chunk[:, 0, 0:1], 0.0))
            step(ve.tensor_tensor_scan(m_chunk[:, 1, 0:NC], last_of(8, True), last_of(3, True), 0.0, ALU.max, ALU.add))
            step(ve.tensor_copy(m_chunk[:, 0, 1:NC], m_chunk[:, 1, 0:NC - 1]))
            step(ve.tensor_tensor(m_chunk[:, 1, NC:NC + NB], last_of(8, False), m_chunk[:, 0, NC:NC + NB], ALU.max))
            step(ve.tensor_tensor(m_chunk[:, 1, NC:NC + NB], m_chunk[:, 1, NC:NC + NB], last_of(3, False), ALU.add))

            def both(out, x, y, op):
                for t0, t1_, c0, n in ((0, NP_, 0, NC), (NP_, T, NC, NB)):
                    w = (t1_ - t0) // n
                    ins_ = ve.tensor_tensor(rows[:, out, t0:t1_].rearrange("p (c t) -> p c t", c=n),
                                            rows[:, x, t0:t1_].rearrange("p (c t) -> p c t", c=n),
                                            y(c0, n).unsqueeze(2).broadcast_to([MH, n, w]), op)
                return ins_

            def m_before(c0, n):
                return m_chunk[:, 0, c0:c0 + n]

            step(both(9, 8, m_before, ALU.max))
            step(ve.tensor_scalar(rows[:, 4, :], rows[:, 9, :], -1.0, None, ALU.mult))
            both(5, 4, m_before, ALU.add)
            ve.tensor_tensor(rows[:, 6, :], rows[:, 4, :], rows[:, 3, :], ALU.subtract)
            both(7, 2, lambda c0, n: last_of(4, c0 == 0), ALU.add).then_inc(mexpo_ready, 1)

            bk = take("L1at")
            ve.tensor_copy(a_tok[:, 0:2], bk[:, 0:4 * MH].rearrange("p (t a h) -> p t a h", t=2, a=2))
            free_step(ve.tensor_copy(a_tok[0:NSM, 2], bk[0:NSM, 4 * MH:6 * MH].rearrange("p (a h) -> p a h", a=2)), "L1at")
            for j in range(4):
                ve.wait_ge(*copied(f"L1q{j}"))
                bk = take(f"L1wb{j}")
                for a in range(2):
                    r = slice(64 * a, 64 * a + 64)
                    ve.tensor_tensor(qwz[r, 2 * j + a, :], qz[r, 2 * j + a, :], bk[r, 0:T], ALU.mult).then_inc(qw_ready, 1)
                ve.tensor_copy(eb[:, j, 0:NC], bk[:, L - 1:NP_:L])
                free_step(ve.tensor_copy(eb[:, j, NC:NC + NB], bk[:, NP_ + NS - 1:T:NS]), f"L1wb{j}")
            ve.wait_ge(kz_zero, 2)
            for tt in range(TT):
                bk = take(f"L1kt{tt}")

                def weighted(c, lo, hi):
                    w = a_tok[lo:hi, tt, 1, :].unsqueeze(2).broadcast_to([hi - lo, MH, 64])
                    return ve.tensor_tensor(kz[lo:hi, c, :].rearrange("p (h k) -> p h k", h=MH),
                                            bk[lo:hi, :].rearrange("p (h k) -> p h k", h=MH), w, ALU.mult)

                if tt < 2:
                    weighted(2 * tt, 0, 64)
                    free_step(weighted(2 * tt + 1, 64, 128), f"L1kt{tt}")
                else:
                    free_step(weighted(NC, 0, NSM), "L1kt2")

            def weights_of(tt):
                n = TS[tt][1]
                halves = 2 if tt < 2 else 1
                per = MH // halves
                part = (lambda hf: f"{tt}{hf}") if tt < 2 else (lambda hf: "2")
                for hf in range(halves):
                    name = "L1db" + part(hf)
                    a = a_tok[0:n, tt, 0, per * hf:per * (hf + 1)].unsqueeze(2).broadcast_to([n, per, n])
                    free_step(ve.tensor_tensor(dmp[0:n, per * hf:per * (hf + 1), 0:n],
                                               take(name)[0:n, 0:per * n].rearrange("p (h t) -> p h t", h=per), a, ALU.add), name)
                v = dmp[0:n, :, 0:n]
                ve.tensor_scalar(v, v, 0.0, None, ALU.min).then_inc(dmp_ready, 1)
                ve.wait_ge(dexp_ready, tt + 1)
                out, m = (P1[:, tt], causal) if tt < 2 else (P1s, causal_s)
                step(ve.tensor_tensor(out, v, over_heads(m[:, :], MH), ALU.mult))
                for hf in range(halves):
                    name = "L1sc" + part(hf)
                    o = out[:, per * hf:per * (hf + 1), :]
                    free(ve.tensor_tensor(o, o, take(name)[0:n, 0:per * n].rearrange("p (h t) -> p h t", h=per), ALU.mult), name)

            weights_of(0)
            free_step(ve.tensor_copy(n_inc[:, :, :], take("L1nu")[:, 0:48].rearrange("p (j c) -> p j c", j=4)), "L1nu")
            weights_of(1)
            weights_of(2)
            ns_b = n_sm[:, :, :].unsqueeze(3).broadcast_to([P, 4, NB, NS])
            for a in range(2):
                step(ve.tensor_tensor(qn[:, a::2, :].rearrange("p j (b i) -> p j b i", b=NB),
                                      qwz[:, a::2, NP_:T].rearrange("p j (b i) -> p j b i", b=NB), ns_b, ALU.mult))
            step(ve.tensor_tensor(n_new[:, :, :], n_sm[:, :, :], eb[:, :, NC:NC + NB], ALU.mult))
            ve.tensor_tensor(n_new[:, :, :], n_new[:, :, :], n_inc[:, :, NC:NC + NB], ALU.add).then_inc(n_new_ready, 1)
            sample_keys("L1", 0, NB)
            sample_keys("L1", 1, NB)

            def add_memory(C, bk, half):
                v = bk[:, :].rearrange("p (j a v) -> p j a v", j=2, a=2)
                for a in range(2):
                    r = slice(64 * a, 64 * a + 64)
                    o = C[r, 2 * half:2 * half + 2, :]
                    ins_ = ve.tensor_tensor(o, o, v[r, :, a, :], ALU.add)
                return ins_

            for c in range(NC):
                new, old = C1[:, (c + 1) % 2], C1[:, c % 2]
                ve.wait_ge(*full(f"L1up{c}a"))
                if c == 0:
                    step(ve.memset(new, 0.0))
                    step(ve.tensor_copy(n_st[:, 1, :], n_inc[:, :, 0]))
                else:
                    step(ve.tensor_tensor(new, old, eb[:, :, c].unsqueeze(2).broadcast_to([P, 4, MDV]), ALU.mult))
                    step(ve.tensor_tensor(n_st[:, (c + 1) % 2, :], n_st[:, c % 2, :], eb[:, :, c], ALU.mult))
                    step(ve.tensor_tensor(n_st[:, (c + 1) % 2, :], n_st[:, (c + 1) % 2, :], n_inc[:, :, c], ALU.add))
                for half, x in enumerate("ab"):
                    free_step(add_memory(new, take(f"L1up{c}{x}"), half), f"L1up{c}{x}")
                ve.tensor_tensor(n_cols[:, (c + 1) % 2].rearrange("p (j a) m -> p j a m", a=2),
                                 head_col[:, :, :].rearrange("p (j a) m -> p j a m", a=2),
                                 n_st[:, (c + 1) % 2, :].unsqueeze(2).unsqueeze(3).broadcast_to([P, 4, 2, MH]), ALU.mult)\
                    .then_inc(norm_ready, 1)
            ve.tensor_copy(m_chunk[:, 2, 0:1], m_chunk[:, 1, 0:1]).then_inc(norm_ready, 1)
            for b in range(NB):
                C = Cs[:, b % 3]
                ve.wait_ge(S_loaded[b % 3], 16 * (S_LOADS[b % 3] + 2 * (b // 3) + 2))
                ve.wait_ge(*full(f"L1us{b}a"))
                step(ve.tensor_tensor(C, C, eb[:, :, NC + b].unsqueeze(2).broadcast_to([P, 4, MDV]), ALU.mult))
                for half, x in enumerate("ab"):
                    free(add_memory(C, take(f"L1us{b}{x}"), half), f"L1us{b}{x}")
                if b + 2 < NB:
                    sample_keys("L1", b + 2, NB)
            free_step(ve.tensor_copy(rows[:, 8, :], take("L1den")[0:MH, 0:T]), "L1den")
            step(stt(rows[:, 9, :], rows[:, 8, :], -1.0, rows[:, 8, :], ALU.mult, ALU.max))
            step(ve.tensor_tensor(rows[:, 9, :], rows[:, 9, :], rows[:, 6, :], ALU.max))
            step(ve.reciprocal(rows[:, 9, :], rows[:, 9, :]))
            free_step(ve.tensor_tensor(rows[:, 0, :], take("L1ns")[0:MH, 0:T], rows[:, 9, :], ALU.mult), "L1ns")
            step(ve.tensor_tensor(rows[:, 0, :], rows[:, 0, :], rows[:, 9, :], ALU.mult))
            ve.tensor_scalar(rows[:, 0, :], rows[:, 0, :], 1.0 / MDV, EPS, ALU.mult, ALU.add).then_inc(mean_ready, 1)
            ve.wait_ge(mean_ready, 2)
            ve.wait_ge(rowx_ready, 2)
            polish(rows[:, 0, :], rows[:, 1, :], rows[:, 2, :], step)
            ve.tensor_tensor(rows[:, 0, :], rows[:, 1, :], rows[:, 9, :], ALU.mult).then_inc(f_ready, 1)
            gated("L1", num, MH, 1, 44)
            residual("L1w", range(KT))

            for i in range(3):
                ve.wait_ge(S_stored[i], 16 * 3 * S_LOADS[i])
            ve.wait_ge(prompt_C_stored, 32)
            ve.memset(h_tok[:, 2, :], 0.0).then_inc(tok_cleared, 1)
            ve.memset(x_acc[:, 2, :], 0.0)
            ve.memset(selT[:, :], 0.0).then_inc(pad_zero, 1)
            step(ve.memset(lg[:, :, :], 0.0))
            step(ve.memset(chosen[:, :, :], 0.0))
            norm(3, "Mss")
            bk = take("Mlog")
            ve.tensor_tensor(lg[:, 0:2, :], bk[:, 0:2 * NE].rearrange("p (t e) -> p t e", t=2),
                             b_rt[:, :].unsqueeze(1).broadcast_to([P, 2, NE]), ALU.add)
            free_step(ve.tensor_tensor(lg[0:NSM, 2, :], bk[0:NSM, 2 * NE:3 * NE], b_rt[0:NSM, :], ALU.add), "Mlog")

            def spread(col):
                c = col if len(col.shape) == 3 else col.unsqueeze(2)
                return c.broadcast_to([P, TT, NE])

            step(ve.tensor_reduce(st[:, 0, :], lg[:, :, :], AX_X, ALU.max))
            ve.tensor_tensor(lg[:, :, :], lg[:, :, :], spread(st[:, 0, :]), ALU.subtract).then_inc(logit_ready, 1)
            ve.wait_ge(prob_ready, 1)
            step(ve.tensor_reduce(st[:, 1, :], pr[:, :, :], AX_X, ALU.add))
            step(ve.reciprocal(st[:, 1, :], st[:, 1, :]))
            step(ve.tensor_tensor(pr[:, :, :], pr[:, :, :], spread(st[:, 1, :]), ALU.mult))
            for tt in range(TT):
                step(ve.max(top_p[:, tt, :], pr[:, tt, :]))
                step(ve.max_index(top_i[:, tt, :], top_p[:, tt, :], pr[:, tt, :]))
            step(ve.tensor_copy(top_f[:, :, :], top_i[:, :, :]))
            e_no = expert_no[:, :].unsqueeze(1).broadcast_to([P, TT, NE])
            step(ve.tensor_tensor(oh1[:, :, :], e_no, spread(top_f[:, :, 0:1]), ALU.is_equal))
            step(ve.tensor_tensor(oh2[:, :, :], e_no, spread(top_f[:, :, 1:2]), ALU.is_equal))
            ve.tensor_tensor(chosen[:, 0:2, :], oh1[:, 0:2, :], oh2[:, 0:2, :], ALU.add)
            ve.tensor_tensor(chosen[0:NSM, 2, :], oh1[0:NSM, 2, :], oh2[0:NSM, 2, :], ALU.add).then_inc(chosen_ready, 1)
            def copy_residual(kts):
                for kt in kts:
                    bk = take(f"Mx{kt}")
                    ve.tensor_copy(x_acc[:, 0:2, kt * P:(kt + 1) * P], bk[:, 0:2 * P].rearrange("p (a b) -> p a b", a=2))
                    free(ve.tensor_copy(x_acc[0:NSM, 2, kt * P:(kt + 1) * P], bk[0:NSM, 2 * P:3 * P]), f"Mx{kt}")

            copy_residual((0, 1, 3))
            bk = take("Mrank")
            stt(place[:, :, :], bk[:, 0:TT * NE].rearrange("p (t e) -> p t e", t=TT), BIG, chosen[:, :, :], ALU.add, ALU.mult)
            free_step(ve.tensor_copy(count[:, :], bk[:, TT * NE:(TT + 1) * NE]), "Mrank")
            step(ve.tensor_scalar(place[:, :, :], place[:, :, :], -BIG, None, ALU.add))
            pos3 = tab_pos[:, :].rearrange("p (i t) -> p t i", t=TT)
            step(ve.tensor_copy(pos3[:, :, 0:NE], place[:, :, :]))

            def select(at, ready):
                for tt in range(TT):
                    ins_ = ve.tensor_scalar(sel[:, tt, :], slot_no[:, :], tab_pos[:, at(tt)], None, ALU.is_equal)
                ins_.then_inc(ready, 1)

            select(lambda tt: slice(tt, tt + 1), sel_ready)
            step(ve.tensor_tensor(st[:, 2, :], top_p[:, :, 0], top_p[:, :, 1], ALU.add))
            step(ve.reciprocal(st[:, 3, :], st[:, 2, :]))
            step(ve.tensor_tensor(oh1[:, :, :], oh1[:, :, :], spread(top_p[:, :, 0:1]), ALU.mult))
            step(ve.tensor_tensor(oh2[:, :, :], oh2[:, :, :], spread(top_p[:, :, 1:2]), ALU.mult))
            step(ve.tensor_tensor(gates[:, :, :], oh1[:, :, :], oh2[:, :, :], ALU.add))
            step(ve.tensor_tensor(gates[:, :, :], gates[:, :, :], spread(st[:, 3, :]), ALU.mult))
            gate3 = tab_gate[:, :].rearrange("p (i t) -> p t i", t=TT)
            step(ve.tensor_copy(gate3[:, :, 0:NE], gates[:, :, :]))
            step(ve.tensor_tensor(flag[:, :, :], count[:, :].unsqueeze(1).broadcast_to([P, 2, NE]), cand_skip[:, :, :], ALU.is_gt))
            f16 = flag[:, :, :].rearrange("p k e -> p (k e)")
            o16 = order[:, :, :].rearrange("p k e -> p (k e)")
            e16 = cand_e[:, :, :].rearrange("p k e -> p (k e)")
            step(ve.tensor_tensor_scan(o16, ones[:, 0:2 * NE], f16, 0.0, ALU.mult, ALU.add))
            step(ve.tensor_scalar(tab_f[:, 15:16], o16[:, 2 * NE - 1:2 * NE], float(NE), None, ALU.add))
            step(ve.tensor_tensor(o16, o16, f16, ALU.mult))
            step(ve.tensor_tensor(pick[:, :, :], o16.unsqueeze(1).broadcast_to([P, MORE, 2 * NE]),
                                  more_no[:, :].unsqueeze(2).broadcast_to([P, MORE, 2 * NE]), ALU.is_equal))

            def picked_value(out, v16):
                step(ve.tensor_tensor(picked[:, :, :], pick[:, :, :], v16.unsqueeze(1).broadcast_to([P, MORE, 2 * NE]), ALU.mult))
                step(ve.tensor_reduce(out, picked[:, :, :], AX_X, ALU.add))

            step(ve.tensor_copy(tab_f[:, 0:NE], expert_no[:, :]))
            step(ve.memset(tab_f[:, NE + MORE:15], 0.0))
            picked_value(tab_f[:, NE:NE + MORE], e16)
            for tt in range(TT):
                step(ve.tensor_tensor(cand_v[:, :, :], place[:, tt, :].unsqueeze(1).broadcast_to([P, 2, NE]), cand_skip[:, :, :], ALU.subtract))
                picked_value(pos3[:, tt, NE:NE + MORE], cand_v[:, :, :].rearrange("p k e -> p (k e)"))
                step(ve.tensor_copy(cand_v[:, :, :], gates[:, tt, :].unsqueeze(1).broadcast_to([P, 2, NE])))
                picked_value(gate3[:, tt, NE:NE + MORE], cand_v[:, :, :].rearrange("p k e -> p (k e)"))
            ve.tensor_copy(tab_i[:, :], tab_f[:, :]).then_inc(table_ready, 1)

            def tokens_lo(half, bk):
                o = slice(4 * half, 4 * half + 4)
                return ve.tensor_tensor(xg_lo[:, o, :], bk[:, 0:4 * CAP].rearrange("p (k c) -> p k c", k=4),
                                        xg_hi[:, o, :].bitcast(F32), ALU.subtract)

            for half in range(2):
                bk = take(f"Mga{half}")
                ve.wait_ge(hi_ready, half + 1)
                free(tokens_lo(half, bk), f"Mga{half}")
            copy_residual((2, 4, 5, 6, 7))
            ve.wait_ge(table_ready, 1)
            n_items = ve.value_load(tab_i[0:1, 15:16], min_val=NE, max_val=NE + MORE)

            def add_piece(n, i, b, k):
                tt, half = n // 2, n % 2
                m = TS[tt][1]
                ve.wait_ge(*loop_full(b, k, i))
                o = x_acc[0:m, tt, half * 512:(half + 1) * 512]
                ve.tensor_tensor(o, o, psum[b][0:m, :], ALU.add).then_inc(bank_free[b], 1)

            def turned_lo(nth, i):
                ve.wait_ge(hi_ready, i * HI_TURNS + (2 + nth + 1))
                ve.tensor_tensor(aT_lo[:, :, :], psum[TB][:, 0:4 * CAP].rearrange("p (f c) -> p f c", f=4),
                                 aT_hi[:, :, :].bitcast(F32), ALU.subtract).then_inc(bank_free[TB], 1)

            with ve.Fori(0, n_items) as i:
                for j in range(PER):
                    src, s = expert_slot(j)
                    ve.wait_ge(whi_ready, i * PER + (j + 1))
                    ve.tensor_tensor(w_lo[:, j % SPLIT, :], src, w_hi[:, j % SPLIT, :].bitcast(F32), ALU.subtract)\
                        .then_inc(wlo_ready, 1)
                    due = expert_order[j - SPLIT] if j >= SPLIT else None
                    if due and due[0] == "g" and due[2] == 1 and due[1]:
                        turned_lo(due[1] - 1, i)
                    if due and due[0] == "u" and due[2] == 1:
                        t = due[1]
                        b = UB[t % 2]
                        ve.wait_ge(*loop_before(GB[t % 2], t // 2 + 1, i))
                        ve.wait_ge(*loop_full(b, t // 2, i))
                        ve.tensor_tensor(act[:, :], sg[:, t % 2, :], psum[b][0:CAP, :], ALU.mult).then_inc(bank_free[b], 1)
                        if t:
                            add_piece(t - 1, i, MB, t - 1)
                    if j == PER // 2:
                        for tt in range(TT):
                            ins_ = ve.tensor_scalar(selg[:, tt, :], slot_no[:, :], tab_pos[:, bass.ds(i * TT + tt, 1)],
                                                    tab_gate[:, bass.ds(i * TT + tt, 1)], ALU.is_equal, ALU.mult)
                        ins_.then_inc(selg_ready, 1)
                        select(lambda tt: bass.ds(i * TT + (TT + tt), 1), sel_ready)
                turned_lo(STEPS - 1, i)
                ve.wait_ge(*loop_full(MB, 6, i))
                ve.tensor_copy(selT[:, :], psum[MB][0:CAP, 0:TT * P]).then_inc(bank_free[MB], 1)
                for half in range(2):
                    ve.wait_ge(hi_ready, i * HI_TURNS + (2 + STEPS + half + 1))
                    tokens_lo(half, psum[GAB[half]]).then_inc(bank_free[GAB[half]], 1)
            for n in range(6):
                add_piece(n, n_items, (MB, TB)[n % 2], n // 2)

            ve.wait_ge(fsq_ready, 3)
            ve.tensor_scalar(st[:, 4, :], st[:, 4, :], 1.0 / D, EPS, ALU.mult, ALU.add).then_inc(fmean_ready, 1)
            ve.wait_ge(fmean_ready, 1)
            ve.wait_ge(finv_ready, 1)
            polish(st[:, 4, :], st[:, 5, :], st[:, 3, :], step)
            for tt, (t0, n) in enumerate(TS):
                stt(x_acc[0:n, tt, :], x_acc[0:n, tt, :], st[0:n, 5, tt:tt + 1], g_final[0:n, :], ALU.mult, ALU.mult)\
                    .then_inc(out_ready, 1)


_INS = ["x_prompt", "x_sample", "state_gla_S", "state_mlstm_C", "state_mlstm_n", "state_mlstm_m",
        "norm_mix", "norm_ffn", "norm_final", "gla_w_in", "gla_w_a2", "gla_b_a", "gla_g_norm", "gla_w_out",
        "mlstm_w_in", "mlstm_b_gate", "mlstm_g_norm", "mlstm_w_out", "ffn_w_gu", "ffn_w_down",
        "moe_w_router", "moe_b_router", "moe_w_gu", "moe_w_down"]
_OUTS = [(1, NP_, D), (NB, NS, D), (1, 1, GH, P, GDV), (1, 1, MH, 64, MDV), (1, 1, MH, 64), (1, 1, MH),
         (1, NB, GH, P, GDV), (1, NB, MH, 64, MDV), (1, NB, MH, 64), (1, NB, MH)]


def kernel(**inputs):
    import numpy as _np
    import concourse.bacc as _bacc
    from concourse import mybir as _mybir
    from concourse.bass_utils import run_bass_kernel_spmd as _run

    nc = _bacc.Bacc("TRN2", target_bir_lowering=False, num_devices=1)
    arrays, ins, outs = {}, {}, []
    for name in _INS:
        a = _np.ascontiguousarray(inputs[name])
        arrays[f"in_{name}_dram"] = a
        ins[name] = nc.dram_tensor(f"in_{name}_dram", a.shape, _mybir.dt.from_np(a.dtype), kind="ExternalInput").ap()
    for i, shape in enumerate(_OUTS):
        outs.append(nc.dram_tensor(f"out_{i}_dram", shape, _mybir.dt.float32, kind="ExternalOutput").ap())
    trunk_kernel(nc, ins, outs)
    r = _run(nc, [arrays], core_ids=[0])
    return tuple(r.results[0][f"out_{i}_dram"] for i in range(len(_OUTS)))
```
